# Optimizing a Trainium2 kernel written in Bass

```python
import math
import jax, jax.numpy as jnp
from jax import lax
import numpy as np

D_MODEL = 1024
BATCH = 1
SEQ = 256
DEPTH = 2

N_MIXERS = 2
N_SSD = (DEPTH + 1) // 2
N_FOX = DEPTH // 2
EPS = 1e-6

SSD_EXPAND = 2
SSD_D_INNER = SSD_EXPAND * D_MODEL
SSD_HEAD_DIM = 64
SSD_HEADS = SSD_D_INNER // SSD_HEAD_DIM
SSD_GROUPS = 4
SSD_HPG = SSD_HEADS // SSD_GROUPS
SSD_STATE = 128
SSD_CONV = 4
SSD_CHUNK = 128
SSD_CONV_DIM = SSD_D_INNER + 2 * SSD_GROUPS * SSD_STATE
SSD_IN_DIM = SSD_D_INNER + SSD_CONV_DIM + SSD_HEADS

FOX_HEAD_DIM = 64
FOX_HEADS = D_MODEL // FOX_HEAD_DIM
FOX_D = FOX_HEADS * FOX_HEAD_DIM
FOX_IN_DIM = 4 * FOX_D + FOX_HEADS
Q_BLOCK = 128

D_FF = 2816
FFN_CONV = 3


def rmsnorm(x, g):
    xf = x.astype(jnp.float32)
    y = xf * lax.rsqrt(jnp.mean(xf * xf, axis=-1, keepdims=True) + EPS)
    return (y * g.astype(jnp.float32)).astype(x.dtype)

def causal_dwconv(x, w, b):
    k_w, c = w.shape
    y = lax.conv_general_dilated(x, w[:, None, :].astype(x.dtype), window_strides=(1,),
                                 padding=[(k_w - 1, 0)],
                                 dimension_numbers=('NWC', 'WIO', 'NWC'),
                                 feature_group_count=c)
    return y + b.astype(x.dtype)

def ssd_chunked(xs, dt, a, bm, cm):
    bsz, s_len = xs.shape[0], xs.shape[1]
    nc, l_c = s_len // SSD_CHUNK, SSD_CHUNK
    x = xs.reshape(bsz, nc, l_c, SSD_GROUPS, SSD_HPG, SSD_HEAD_DIM)
    dtc = dt.reshape(bsz, nc, l_c, SSD_GROUPS, SSD_HPG)
    bc = bm.reshape(bsz, nc, l_c, SSD_GROUPS, SSD_STATE)
    cc = cm.reshape(bsz, nc, l_c, SSD_GROUPS, SSD_STATE)
    da = jnp.moveaxis(dtc * a.reshape(SSD_GROUPS, SSD_HPG), 2, -1)
    a_cs = jnp.cumsum(da, axis=-1)
    xdt = x * dtc[..., None]
    causal = jnp.tril(jnp.ones((l_c, l_c), dtype=bool))
    decay = jnp.exp(jnp.where(causal, a_cs[..., :, None] - a_cs[..., None, :], -jnp.inf))
    cb = jnp.einsum('bclgn,bcsgn->bcgls', cc, bc)
    y_diag = jnp.einsum('bcgrls,bcsgrp->bclgrp', cb[:, :, :, None] * decay, xdt)
    decay_states = jnp.exp(a_cs[..., -1:] - a_cs)
    states = jnp.einsum('bclgn,bcgrl,bclgrp->bcgrpn', bc, decay_states, xdt).astype(jnp.float32)
    chunk_decay = jnp.exp(a_cs[..., -1])

    def step(h, inp):
        st, dec = inp
        return h * dec[..., None, None] + st, h

    h0 = jnp.zeros((bsz, SSD_GROUPS, SSD_HPG, SSD_HEAD_DIM, SSD_STATE), jnp.float32)
    _, prev = lax.scan(step, h0, (jnp.moveaxis(states, 1, 0), jnp.moveaxis(chunk_decay, 1, 0)))
    prev = jnp.moveaxis(prev, 0, 1)
    y_off = jnp.einsum('bclgn,bcgrpn,bcgrl->bclgrp', cc, prev, jnp.exp(a_cs))
    return (y_diag + y_off).reshape(bsz, s_len, SSD_HEADS, SSD_HEAD_DIM).astype(xs.dtype)

def mamba2_mixer(h, w_in, conv_w, conv_b, dt_bias, a_log, d_skip, norm_g, w_out):
    bsz, s_len, _ = h.shape
    proj = h @ w_in
    z = proj[..., :SSD_D_INNER]
    xbc = proj[..., SSD_D_INNER:SSD_D_INNER + SSD_CONV_DIM]
    dt_raw = proj[..., SSD_D_INNER + SSD_CONV_DIM:]
    xbc = jax.nn.silu(causal_dwconv(xbc, conv_w, conv_b))
    gn = SSD_GROUPS * SSD_STATE
    xs = xbc[..., :SSD_D_INNER].reshape(bsz, s_len, SSD_HEADS, SSD_HEAD_DIM)
    bm = xbc[..., SSD_D_INNER:SSD_D_INNER + gn].reshape(bsz, s_len, SSD_GROUPS, SSD_STATE)
    cm = xbc[..., SSD_D_INNER + gn:].reshape(bsz, s_len, SSD_GROUPS, SSD_STATE)
    dt = jax.nn.softplus((dt_raw + dt_bias).astype(jnp.float32))
    a = -jnp.exp(a_log.astype(jnp.float32))
    y = ssd_chunked(xs, dt, a, bm, cm) + xs * d_skip[:, None]
    y = y.reshape(bsz, s_len, SSD_D_INNER)
    yz = (y * jax.nn.silu(z)).astype(jnp.float32).reshape(bsz, s_len, SSD_GROUPS, SSD_D_INNER // SSD_GROUPS)
    yz = yz * lax.rsqrt(jnp.mean(yz * yz, axis=-1, keepdims=True) + EPS)
    y = (yz.reshape(bsz, s_len, SSD_D_INNER) * norm_g.astype(jnp.float32)).astype(h.dtype)
    return y @ w_out

def fox_attention(h, w_in, b_f, q_norm_g, k_norm_g, w_out):
    bsz, s_len, _ = h.shape
    proj = h @ w_in
    q = rmsnorm(proj[..., :FOX_D].reshape(bsz, s_len, FOX_HEADS, FOX_HEAD_DIM), q_norm_g)
    k = rmsnorm(proj[..., FOX_D:2 * FOX_D].reshape(bsz, s_len, FOX_HEADS, FOX_HEAD_DIM), k_norm_g)
    v = proj[..., 2 * FOX_D:3 * FOX_D].reshape(bsz, s_len, FOX_HEADS, FOX_HEAD_DIM)
    gate = proj[..., 3 * FOX_D:4 * FOX_D]
    log_f = jax.nn.log_sigmoid((proj[..., 4 * FOX_D:] + b_f).astype(jnp.float32))
    cum = jnp.transpose(jnp.cumsum(log_f, axis=1), (0, 2, 1))
    q, k, v = (jnp.transpose(t, (0, 2, 1, 3)) for t in (q, k, v))
    scale = FOX_HEAD_DIM ** -0.5
    outs = []
    for i in range(s_len // Q_BLOCK):
        qs, qe = i * Q_BLOCK, (i + 1) * Q_BLOCK
        sc = jnp.einsum('bhqd,bhkd->bhqk', q[:, :, qs:qe], k[:, :, :qe]).astype(jnp.float32) * scale
        sc = sc + cum[:, :, qs:qe, None] - cum[:, :, None, :qe]
        mask = (qs + jnp.arange(Q_BLOCK))[:, None] >= jnp.arange(qe)[None, :]
        p = jax.nn.softmax(jnp.where(mask, sc, -jnp.inf), axis=-1)
        outs.append(jnp.einsum('bhqk,bhkd->bhqd', p.astype(v.dtype), v[:, :, :qe]))
    o = jnp.transpose(jnp.concatenate(outs, axis=2), (0, 2, 1, 3)).reshape(bsz, s_len, FOX_D)
    return (o * jax.nn.sigmoid(gate)) @ w_out

def conv_glu_ffn(h, w_up, conv_w, conv_b, w_down):
    u = h @ w_up
    gate = causal_dwconv(u[..., :D_FF], conv_w, conv_b)
    return (jax.nn.silu(gate) * u[..., D_FF:]) @ w_down

def first_inputs(seed: int = 0) -> dict:
    key = jax.random.key(seed)
    ks = jax.random.split(key, 24)
    f32 = jnp.float32

    def nrm(k, shape, scale):
        return jax.random.normal(k, shape, f32) * scale

    res_scale = (2 * DEPTH) ** -0.5
    dt_init = jnp.exp(jax.random.uniform(ks[4], (N_SSD, SSD_HEADS), f32, math.log(1e-3), math.log(1e-1)))
    return {
        'x': nrm(ks[0], (BATCH, SEQ, D_MODEL), 1.0),
        'mix_norm_g': 1.0 + nrm(ks[1], (DEPTH, D_MODEL), 0.02),
        'ffn_norm_g': 1.0 + nrm(ks[2], (DEPTH, D_MODEL), 0.02),
        'ssd_w_in': nrm(ks[3], (N_SSD, D_MODEL, SSD_IN_DIM), D_MODEL ** -0.5),
        'ssd_conv_w': nrm(ks[5], (N_SSD, SSD_CONV, SSD_CONV_DIM), SSD_CONV ** -0.5),
        'ssd_conv_b': nrm(ks[6], (N_SSD, SSD_CONV_DIM), 0.02),
        'ssd_dt_bias': dt_init + jnp.log(-jnp.expm1(-dt_init)),
        'ssd_a_log': jnp.log(jax.random.uniform(ks[7], (N_SSD, SSD_HEADS), f32, 1.0, 16.0)),
        'ssd_d': 1.0 + nrm(ks[8], (N_SSD, SSD_HEADS), 0.1),
        'ssd_norm_g': 1.0 + nrm(ks[9], (N_SSD, SSD_D_INNER), 0.02),
        'ssd_w_out': nrm(ks[10], (N_SSD, SSD_D_INNER, D_MODEL), SSD_D_INNER ** -0.5 * res_scale),
        'fox_w_in': nrm(ks[11], (N_FOX, D_MODEL, FOX_IN_DIM), D_MODEL ** -0.5),
        'fox_b_f': jax.random.uniform(ks[12], (N_FOX, FOX_HEADS), f32, 2.0, 6.0),
        'fox_q_norm_g': 1.0 + nrm(ks[13], (N_FOX, FOX_HEAD_DIM), 0.02),
        'fox_k_norm_g': 1.0 + nrm(ks[14], (N_FOX, FOX_HEAD_DIM), 0.02),
        'fox_w_out': nrm(ks[15], (N_FOX, FOX_D, D_MODEL), FOX_D ** -0.5 * res_scale),
        'ffn_w_up': nrm(ks[16], (DEPTH, D_MODEL, 2 * D_FF), D_MODEL ** -0.5),
        'ffn_conv_w': nrm(ks[17], (DEPTH, FFN_CONV, D_FF), FFN_CONV ** -0.5),
        'ffn_conv_b': nrm(ks[18], (DEPTH, D_FF), 0.02),
        'ffn_w_down': nrm(ks[19], (DEPTH, D_FF, D_MODEL), D_FF ** -0.5 * res_scale),
        'final_norm_g': 1.0 + nrm(ks[20], (D_MODEL,), 0.02),
    }

def first_block(x, mix_norm_g, ffn_norm_g,
              ssd_w_in, ssd_conv_w, ssd_conv_b, ssd_dt_bias, ssd_a_log, ssd_d, ssd_norm_g, ssd_w_out,
              fox_w_in, fox_b_f, fox_q_norm_g, fox_k_norm_g, fox_w_out,
              ffn_w_up, ffn_conv_w, ffn_conv_b, ffn_w_down, final_norm_g):
    h = x
    for i in range(DEPTH):
        hn = rmsnorm(h, mix_norm_g[i])
        j = i // N_MIXERS
        if i % N_MIXERS == 0:
            h = h + mamba2_mixer(hn, ssd_w_in[j], ssd_conv_w[j], ssd_conv_b[j], ssd_dt_bias[j],
                                 ssd_a_log[j], ssd_d[j], ssd_norm_g[j], ssd_w_out[j])
        else:
            h = h + fox_attention(hn, fox_w_in[j], fox_b_f[j], fox_q_norm_g[j], fox_k_norm_g[j], fox_w_out[j])
        h = h + conv_glu_ffn(rmsnorm(h, ffn_norm_g[i]), ffn_w_up[i], ffn_conv_w[i], ffn_conv_b[i], ffn_w_down[i])
    return rmsnorm(h, final_norm_g)


DEPTH_2 = 1

N_META = 16
BLOCK = 128
MLA_HEADS = 8
QK_NOPE = 64
QK_ROPE = 32
V_HEAD = 64
Q_LORA = 256
KV_LORA = 128
ROPE_THETA = 10000.0
MLA_WIDTH = MLA_HEADS * V_HEAD
CONV_CH = 512
CONV_K = 31
CONV_WIDTH = CONV_CH
MIX_WIDTH = MLA_WIDTH + CONV_WIDTH
IN_COLS = 2 * CONV_CH + Q_LORA + KV_LORA + QK_ROPE
N_KEYS = 128
N_EXPERTS = N_KEYS * N_KEYS
PEER_HEADS = 8
PEER_DK = 128
PEER_DK_HALF = PEER_DK // 2
PEER_TOPK = 16
PEER_CHUNK = 128
NORM_EPS = 1e-6


def rmsnorm_2(x, g):
    xf = x.astype(jnp.float32)
    y = xf * lax.rsqrt(jnp.mean(xf * xf, axis=-1, keepdims=True) + NORM_EPS)
    return (y * g.astype(jnp.float32)).astype(x.dtype)

def layernorm(x, g, b):
    xf = x.astype(jnp.float32)
    mu = jnp.mean(xf, axis=-1, keepdims=True)
    var = jnp.mean(jnp.square(xf - mu), axis=-1, keepdims=True)
    y = (xf - mu) * lax.rsqrt(var + NORM_EPS)
    return (y * g.astype(jnp.float32) + b.astype(jnp.float32)).astype(x.dtype)

def rope(x, pos):
    half = x.shape[-1] // 2
    freqs = ROPE_THETA ** (-jnp.arange(half, dtype=jnp.float32) / half)
    ang = pos.astype(jnp.float32)[:, None] * freqs[None, :]
    cos = jnp.cos(ang)[None, :, None, :].astype(x.dtype)
    sin = jnp.sin(ang)[None, :, None, :].astype(x.dtype)
    x1, x2 = x[..., :half], x[..., half:]
    return jnp.concatenate([x1 * cos - x2 * sin, x2 * cos + x1 * sin], axis=-1)

def causal_block_attention(q, k, v):
    B, Tp, H, Dq = q.shape
    nb = Tp // BLOCK
    qb = q.reshape(B, nb, BLOCK, H, Dq).transpose(1, 0, 2, 3, 4)
    kpos = jnp.arange(Tp)
    scale = 1.0 / math.sqrt(Dq)

    def one(args):
        qblk, i = args
        s = jnp.einsum('bqhd,bkhd->bhqk', qblk, k).astype(jnp.float32) * scale
        qpos = i * BLOCK + jnp.arange(BLOCK)
        mask = kpos[None, :] <= qpos[:, None]
        s = jnp.where(mask[None, None], s, -jnp.inf)
        p = jax.nn.softmax(s, axis=-1).astype(v.dtype)
        return jnp.einsum('bhqk,bkhd->bqhd', p, v)

    o = lax.map(one, (qb, jnp.arange(nb)))
    return o.transpose(1, 0, 2, 3, 4).reshape(B, Tp, H, v.shape[-1])

def mla_group(c_q, c_kv, k_rope_in, pos, g_q, w_uq, g_kv, w_ukv):
    B, Tp, _ = c_q.shape
    q = (rmsnorm_2(c_q, g_q) @ w_uq).reshape(B, Tp, MLA_HEADS, QK_NOPE + QK_ROPE)
    q = jnp.concatenate([q[..., :QK_NOPE], rope(q[..., QK_NOPE:], pos)], axis=-1)
    kv = (rmsnorm_2(c_kv, g_kv) @ w_ukv).reshape(B, Tp, MLA_HEADS, QK_NOPE + V_HEAD)
    k_nope, v = kv[..., :QK_NOPE], kv[..., QK_NOPE:]
    k_r = rope(k_rope_in[:, :, None, :], pos)
    k = jnp.concatenate([k_nope, jnp.broadcast_to(k_r, (B, Tp, MLA_HEADS, QK_ROPE))], axis=-1)
    o = causal_block_attention(q, k, v)
    return o.reshape(B, Tp, MLA_WIDTH)

def conv_group(a, b, conv_w, conv_b, g_ln, b_ln):
    h = a * jax.nn.sigmoid(b)
    h = lax.conv_general_dilated(h, conv_w[:, None, :].astype(h.dtype), window_strides=(1,),
                                 padding=[(CONV_K - 1, 0)],
                                 dimension_numbers=('NWC', 'WIO', 'NWC'),
                                 feature_group_count=CONV_CH) + conv_b
    h = layernorm(h, g_ln, b_ln)
    return jax.nn.silu(h)

def peer_ffn(xn, wq, keys, u_tab, v_tab):
    B, Tp, D = xn.shape
    xc = xn.reshape(-1, PEER_CHUNK, D)
    K = PEER_TOPK

    def one(xb):
        C = xb.shape[0]
        q = (xb @ wq).reshape(C, PEER_HEADS, 2, PEER_DK_HALF)
        s = jnp.einsum('chpd,hpnd->chpn', q, keys).astype(jnp.float32)
        sv, si = lax.top_k(s, K)
        cand = sv[:, :, 0, :, None] + sv[:, :, 1, None, :]
        cidx = si[:, :, 0, :, None] * N_KEYS + si[:, :, 1, None, :]
        top_s, sel = lax.top_k(cand.reshape(C, PEER_HEADS, K * K), K)
        eidx = jnp.take_along_axis(cidx.reshape(C, PEER_HEADS, K * K), sel, axis=-1)
        g = jax.nn.softmax(top_s, axis=-1)
        u = u_tab[eidx]
        act = jax.nn.gelu(jnp.einsum('chkd,cd->chk', u, xb).astype(jnp.float32), approximate=False)
        w = (g * act).astype(xb.dtype)
        return jnp.einsum('chk,chkd->cd', w, v_tab[eidx])

    return lax.map(one, xc).reshape(B, Tp, D)

def second_inputs(seed: int = 0) -> dict:
    key = jax.random.key(seed)
    ks = jax.random.split(key, 24)
    f32 = jnp.float32
    L, D = DEPTH_2, D_MODEL

    def nrm(k, shape, scale):
        return jax.random.normal(k, shape, f32) * scale

    def gain(k, shape):
        return 1.0 + 0.02 * jax.random.normal(k, shape, f32)

    return {
        "x": jax.random.normal(ks[0], (BATCH, SEQ, D), f32),
        "meta": nrm(ks[1], (N_META, D), 1.0),
        "g_mix_norm": gain(ks[2], (L, D)),
        "w_in": nrm(ks[3], (L, D, IN_COLS), D ** -0.5),
        "g_q": gain(ks[4], (L, Q_LORA)),
        "w_uq": nrm(ks[5], (L, Q_LORA, MLA_HEADS * (QK_NOPE + QK_ROPE)), Q_LORA ** -0.5),
        "g_kv": gain(ks[6], (L, KV_LORA)),
        "w_ukv": nrm(ks[7], (L, KV_LORA, MLA_HEADS * (QK_NOPE + V_HEAD)), KV_LORA ** -0.5),
        "conv_w": nrm(ks[8], (L, CONV_K, CONV_CH), CONV_K ** -0.5),
        "conv_b": nrm(ks[9], (L, CONV_CH), 0.02),
        "g_conv_ln": gain(ks[10], (L, CONV_CH)),
        "b_conv_ln": nrm(ks[11], (L, CONV_CH), 0.02),
        "g_out_attn": gain(ks[12], (L, MLA_WIDTH)),
        "g_out_conv": gain(ks[13], (L, CONV_WIDTH)),
        "w_out": nrm(ks[14], (L, MIX_WIDTH, D), MIX_WIDTH ** -0.5),
        "g_ffn_norm": gain(ks[15], (L, D)),
        "peer_wq": nrm(ks[16], (L, D, PEER_HEADS * PEER_DK), D ** -0.5),
        "peer_keys": nrm(ks[17], (L, PEER_HEADS, 2, N_KEYS, PEER_DK_HALF), PEER_DK_HALF ** -0.5),
        "peer_u": nrm(ks[18], (L, N_EXPERTS, D), D ** -0.5),
        "peer_v": nrm(ks[19], (L, N_EXPERTS, D), (PEER_HEADS * PEER_TOPK) ** -0.5),
        "g_final": gain(ks[20], (D,)),
    }

def second_block(x, meta, g_mix_norm, w_in, g_q, w_uq, g_kv, w_ukv, conv_w, conv_b, g_conv_ln, b_conv_ln,
              g_out_attn, g_out_conv, w_out, g_ffn_norm, peer_wq, peer_keys, peer_u, peer_v, g_final):
    B, S, D = x.shape
    T = N_META + S
    Tp = ((T + BLOCK - 1) // BLOCK) * BLOCK
    h = jnp.concatenate([jnp.broadcast_to(meta.astype(x.dtype)[None], (B, N_META, D)), x,
                         jnp.zeros((B, Tp - T, D), x.dtype)], axis=1)
    pos = jnp.arange(Tp, dtype=jnp.int32)

    c0 = 2 * CONV_CH
    c1 = c0 + Q_LORA
    c2 = c1 + KV_LORA
    for l in range(DEPTH_2):
        hn = rmsnorm_2(h, g_mix_norm[l])
        z = hn @ w_in[l]
        conv_out = conv_group(z[..., :CONV_CH], z[..., CONV_CH:c0], conv_w[l], conv_b[l],
                              g_conv_ln[l], b_conv_ln[l])
        attn_out = mla_group(z[..., c0:c1], z[..., c1:c2], z[..., c2:], pos,
                             g_q[l], w_uq[l], g_kv[l], w_ukv[l])
        mixed = jnp.concatenate([rmsnorm_2(attn_out, g_out_attn[l]),
                                 rmsnorm_2(conv_out, g_out_conv[l])], axis=-1)
        h = h + mixed @ w_out[l]
        h = h + peer_ffn(rmsnorm_2(h, g_ffn_norm[l]), peer_wq[l], peer_keys[l], peer_u[l], peer_v[l])

    h = rmsnorm_2(h, g_final)
    return h[:, N_META:N_META + S, :]


def setup_inputs(seed=0):
    out = dict(first_inputs(seed))
    for name, value in second_inputs(seed + 1).items():
        if name != "x":
            out[name + "_2"] = value
    return out


def reference(
    x, mix_norm_g, ffn_norm_g, ssd_w_in, ssd_conv_w, ssd_conv_b, ssd_dt_bias, ssd_a_log, ssd_d,
    ssd_norm_g, ssd_w_out, fox_w_in, fox_b_f, fox_q_norm_g, fox_k_norm_g, fox_w_out, ffn_w_up,
    ffn_conv_w, ffn_conv_b, ffn_w_down, final_norm_g, meta_2, g_mix_norm_2, w_in_2, g_q_2,
    w_uq_2, g_kv_2, w_ukv_2, conv_w_2, conv_b_2, g_conv_ln_2, b_conv_ln_2, g_out_attn_2,
    g_out_conv_2, w_out_2, g_ffn_norm_2, peer_wq_2, peer_keys_2, peer_u_2, peer_v_2, g_final_2,
):
    x = first_block(
        x, mix_norm_g, ffn_norm_g, ssd_w_in, ssd_conv_w, ssd_conv_b, ssd_dt_bias, ssd_a_log,
        ssd_d, ssd_norm_g, ssd_w_out, fox_w_in, fox_b_f, fox_q_norm_g, fox_k_norm_g, fox_w_out,
        ffn_w_up, ffn_conv_w, ffn_conv_b, ffn_w_down, final_norm_g,
    )
    return second_block(
        x, meta_2, g_mix_norm_2, w_in_2, g_q_2, w_uq_2, g_kv_2, w_ukv_2, conv_w_2, conv_b_2,
        g_conv_ln_2, b_conv_ln_2, g_out_attn_2, g_out_conv_2, w_out_2, g_ffn_norm_2, peer_wq_2,
        peer_keys_2, peer_u_2, peer_v_2, g_final_2,
    )


_drawn_inputs = setup_inputs


def setup_inputs(seed=0):
    import zlib

    import numpy as np

    out = dict(_drawn_inputs(seed))
    spreads = {}
    factors = {'mix_norm_g': 3.358,
     'ffn_norm_g': 4.5,
     'ssd_conv_b': 3.243,
     'ssd_norm_g': 4.706,
     'fox_q_norm_g': 8.0,
     'fox_k_norm_g': 8.0,
     'ffn_conv_b': 6.569,
     'g_mix_norm_2': 3.02,
     'g_q_2': 5.916,
     'g_kv_2': 3.88,
     'conv_b_2': 3.1,
     'g_conv_ln_2': 13.636,
     'b_conv_ln_2': 13.439,
     'g_out_attn_2': 16.05,
     'g_out_conv_2': 16.586,
     'g_ffn_norm_2': 32.053,
     'g_final_2': 7.969}
    for name, (base, spread) in spreads.items():
        noise = np.random.default_rng([zlib.crc32(name.encode()), seed]).standard_normal(out[name].shape)
        drawn = base * np.exp(spread * noise) if base else spread * noise
        out[name] = __import__('jax').numpy.asarray(drawn.astype(out[name].dtype))
    for name, factor in factors.items():
        out[name] = (out[name] * factor).astype(out[name].dtype)
    return out
```

```python
import math

import numpy as np
import concourse.bass as bass
from concourse import mybir

F32 = mybir.dt.float32
F32R = mybir.dt.float32r
BF16 = mybir.dt.bfloat16
U32 = mybir.dt.uint32
I32 = mybir.dt.int32
ACT = mybir.ActivationFunctionType
ALU = mybir.AluOpType
AX = mybir.AxisListType

P = 128
D = 1024
KC = D // P
SEQ = 256
META = 16
T2 = META + SEQ
NT = SEQ // P
EPS = 1e-6
UNIT = 2048

INNER = 2048
GROUPS = 4
STATE = 128
HEADS = 32
HPG = 8
HD = 64
XBC_TILES = (INNER + 2 * GROUPS * STATE) // P
FT = 2816 // P

FH = 16
MH = 8
NOPE = 64
ROPE = 32
QD = NOPE + ROPE
CONV_K = 31
CT = 4

PH = 8
NKEY = 128
TOPK = 16

U_BC = 0
U_XS = U_BC + 4
U_Z = U_XS + 8
U_SOUT = U_Z + 8
U_FFN0 = U_SOUT + 8
FFN_UNITS = FT + FT // 2
U_FQ = U_FFN0 + FFN_UNITS
U_FOUT = U_FQ + 16
U_FFN1 = U_FOUT + 4
U_CONV = U_FFN1 + FFN_UNITS
U_CQ = U_CONV + 4
U_CKV = U_CQ + 1
U_MOUT = U_CKV + 1
U_WQ = U_MOUT + 4
U_PEER = U_WQ + 4
PAIRS = NKEY // 2
RING = 3
GT = 8
GROUPS_OF_TOKENS = SEQ // GT

COLS = {}
_n = 0
for _name, _k in (("mix0", 8), ("ffn0", 8), ("mix1", 8), ("ffn1", 8), ("mix2", 8), ("ffn2", 8),
                  ("sconv", XBC_TILES * 5), ("snorm", 16), ("fconv0", FT * 4), ("fconv1", FT * 4),
                  ("cconv", CT * 32), ("gout", 8), ("gq", 2), ("gkv", 1)):
    COLS[_name] = _n
    _n += _k
NCOLS = _n

ROWS = {}
_n = 0
for _name, _k in (("dtb", HEADS), ("alog", HEADS), ("dskip", HEADS), ("bf", FH), ("fqg", HD), ("fkg", HD),
                  ("lng", 512), ("lnb", 512), ("final", D)):
    ROWS[_name] = _n
    _n += _k
NROWS = _n


class Chain:

    def __init__(self, eng, sem):
        self.eng, self.sem, self.n = eng, sem, 0

    def lag(self, ins):
        self.n += 1
        ins.then_inc(self.sem, 1)
        if self.n > 1:
            self.eng.wait_ge(self.sem, self.n - 1)

    def settle(self):
        self.eng.wait_ge(self.sem, self.n)

    def __call__(self, ins):
        ins.then_inc(self.sem, 1)
        self.n += 1
        self.eng.wait_ge(self.sem, self.n)


def build(nc, A, out):
    base = (nc.sbuf_base + 63) // 64 * 64
    place = {"at": base}

    def sb(name, shape, dt=F32, at=None):
        size = int(np.prod(shape[1:])) * (2 if dt == BF16 else 4)
        size = (size + 31) // 32 * 32
        off = place["at"] if at is None else at
        t = nc.alloc_sbuf_tensor_at(name, shape, dt, offset=off)
        if at is None:
            place["at"] += size
        return t

    def sem(name):
        return nc.alloc_semaphore(name)

    raw, hi, lo = [], [], []
    slot_at = {}
    for s in range(2):
        raw.append(sb(f"raw{s}", [P, UNIT]))
    slot_at["raw1"] = place["at"] - UNIT * 4
    for s in range(2):
        hi.append(sb(f"hi{s}", [P, UNIT], F32R))
    slot_at["hi1"] = place["at"] - UNIT * 4
    for s in range(2):
        lo.append(sb(f"lo{s}", [P, UNIT], F32R))
    slot_at["lo1"] = place["at"] - UNIT * 4
    xh = sb("xh", [P, KC, T2], F32R)
    xl = sb("xl", [P, KC, T2], F32R)
    ident = sb("ident", [P, P])
    ones = sb("ones", [P, P])
    tri = sb("tri", [P, P])
    iota = sb("iota", [P, P])
    identb = sb("identb", [P, P], BF16)
    negm = sb("negm", [P, T2], BF16)
    cols = sb("cols", [P, NCOLS])
    stat = sb("stat", [P, 128])
    rs = sb("rs", [P, 3, 32])
    fixed_end = place["at"]
    raw.append(sb("raw2", [P, UNIT]))
    hi.append(sb("hi2", [P, UNIT], F32R))
    lo.append(sb("lo2", [P, UNIT], F32R))
    h = sb("h", [P, NT, D])
    rows = sb("rows", [P, NROWS])
    xn_at = place["at"]
    xn = sb("xn", [P, NT, D])
    oh = sb("oh", [P, 2, 2, SEQ], F32R)
    ol = sb("ol", [P, 2, 2, SEQ], F32R)
    tmp = [sb(f"tmp{i}", [P, 512]) for i in range(4)]
    phase = place["at"]

    def start_phase():
        place["at"] = phase

    cv = [sb(f"cv{i}", [P, 2, SEQ]) for i in range(2)]
    xsf = [sb(f"xsf{i}", [P, 2, SEQ]) for i in range(2)]
    bct = sb("bct", [P, 8, SEQ])
    b_tm = sb("b_tm", [P, GROUPS, STATE])
    x_tm = sb("x_tm", [P, NT, INNER])
    cbm = sb("cbm", [P, NT, P])
    dec = [sb("dec0", [P, HPG, P]), sb("dec1", [P, HPG, P], at=xn_at + 8192)]
    xdt = [sb("xdt0", [P, HPG, HD]), sb("xdt1", [P, HPG, HD], at=xn_at + 12288)]
    xdst = sb("xdst", [P, HPG, HD])
    st_t = sb("st_t", [P, 512])
    y_tm = sb("y_tm", [P, NT, INNER])
    cbm_sq = sb("cbm_sq", [P, 512], at=xn_at + 4096)
    assert place["at"] <= nc.sbuf_usable_end, place["at"]
    sz = tmp[2], tmp[3]
    wdt = sb("wdt", [P, KC, HEADS], at=xn_at + 8192 - 0)
    wdth = sb("wdth", [P, KC, HEADS], F32R, at=xn_at + 8192 + 1024)
    wdtl = sb("wdtl", [P, KC, HEADS], F32R, at=xn_at + 8192 + 2048)
    dtv = sb("dtv", [P, 12, NT, HEADS], at=xn_at)
    start_phase()
    fcv = sb("fcv", [P, SEQ])
    fh32 = sb("fh32", [P, SEQ])
    hdh = sb("hdh", [P, 2, SEQ], F32R)
    hdl = sb("hdl", [P, 2, SEQ], F32R)
    start_phase()
    DA = HD + 2
    fq = sb("fq", [P, NT, FH, DA])
    fk = sb("fk", [P, NT, FH, DA])
    fv = sb("fv", [P, NT, D])
    fg = sb("fg", [P, NT, D])
    qkt = [sb(f"qkt{i}", [P, 4, P]) for i in range(2)]
    pr = [sb(f"pr{i}", [P, 3, P]) for i in range(2)]
    prt = [sb(f"prt{i}", [P, 3, P]) for i in range(2)]
    fst = sb("fst", [P, 8, NT, FH])
    wf = sb("wf", [P, KC, FH])
    wfh = sb("wfh", [P, KC, FH], F32R)
    wfl = sb("wfl", [P, KC, FH], F32R)
    assert place["at"] <= nc.sbuf_usable_end, place["at"]
    start_phase()
    HCW = CONV_K - 1 - META + T2
    hc = sb("hc", [P, CT, HCW])
    ca = sb("ca", [P, CT, SEQ])
    wuq = sb("wuq", [P, 2, MH * QD])
    wukv = sb("wukv", [P, MH * 128])
    mq = sb("mq", [P, NT, MH, QD])
    mk = sb("mk", [P, 3, MH, QD])
    mv = sb("mv", [P, 3, MH, HD])
    cqt = sb("cqt", [P, 2, SEQ])
    ckt = sb("ckt", [P, T2])
    kr = sb("kr", [P, 3, ROPE])
    cs = sb("cs", [P, 3, 2, 16])
    mqt = [sb(f"mqt{i}", [P, SEQ + T2]) for i in range(1)]
    mp = [sb(f"mp{i}", [P, 416]) for i in range(1)]
    mpt = [sb(f"mpt{i}", [P, 5, P]) for i in range(1)]
    hm = sb("hm", [META, D])
    mst = sb("mst", [P, 64])
    assert place["at"] <= nc.sbuf_usable_end, place["at"]
    mix = xn
    start_phase()
    keys = sb("keys", [P, PH, 2 * NKEY])
    qp = sb("qp", [P, PH, SEQ])
    sc = sb("sc", [P, NT, 2 * PH, NKEY])
    cand = sb("cand", [P, NT, PH, TOPK * TOPK])
    sv = sb("sv", [P, NT, 2 * PH, TOPK])
    si = sb("si", [P, NT, 2 * PH, TOPK], U32)
    sif = sb("sif", [P, NT, 2 * PH, TOPK])
    tv = sb("tv", [P, NT, PH, TOPK])
    ts = sb("ts", [P, NT, PH, TOPK], U32)
    tau = sb("tau", [P, NT, PH, TOPK], U32)
    tbu = sb("tbu", [P, NT, PH, TOPK], U32)
    taf = sb("taf", [P, NT, PH, TOPK])
    tbf = sb("tbf", [P, NT, PH, TOPK])
    assert place["at"] <= nc.sbuf_usable_end, place["at"]
    eq = sb("eq", [P, PH * TOPK, TOPK], at=xn_at)
    sif_sel = [sb(f"sel{i}", [P, NT, PH, TOPK], at=xn_at + 8192 + 1024 * i) for i in range(2)]
    place["at"] = fixed_end
    lists_at = fixed_end
    gl = sb("gl", [P, 2, SEQ])
    wgh = sb("wgh", [P, 2, SEQ], F32R)
    wgl = sb("wgl", [P, 2, SEQ], F32R)
    gates = sb("gates", [P, NKEY, SEQ])
    assert place["at"] <= nc.sbuf_usable_end, (place["at"], nc.sbuf_usable_end)
    lst = sb("lst", [P, 3, SEQ], at=lists_at)
    oi = [sb(f"oi{i}", [P, GT, P], at=slot_at[n]) for i, n in enumerate(("hi1", "lo1", "raw1"))]
    oj = [sb(f"oj{i}", [P, GT, P], at=slot_at[n] + GT * P * 4) for i, n in enumerate(("hi1", "lo1", "raw1"))]
    g_at = lists_at + 3 * 2048
    hf = sb("hf", [P, NT, D], at=g_at)
    gfin = sb("gfin", [P, D], at=g_at + 8192)
    fo = sb("fo", [P, NT, D], at=g_at + 16384)

    ps = nc.alloc_psum_tensor("ps", [P, 8, 512], F32)
    h_save = nc.dram_tensor("h_save", (P, NT * D), F32, kind="Internal").ap()

    x_loaded, cols_loaded, rows_loaded, wdt_loaded = sem("x_loaded"), sem("cols_loaded"), sem("rows_loaded"), sem("wdt_loaded")
    raw_in = [sem(f"raw_in{s}") for s in range(RING)]
    hi_done, lo_done, unit_used = sem("hi_done"), sem("lo_done"), sem("unit_used")
    hi_u_done, lo_u_done, hi_v_done, lo_v_done = sem("hi_u_done"), sem("lo_u_done"), sem("hi_v_done"), sem("lo_v_done")
    consts = sem("consts")
    pool_c, dve_c, act_c = sem("pool_chain"), sem("dve_chain"), sem("act_chain")
    ssq_done, xn_ready, xt_filled, x_ready, h_ready = (sem(n) for n in ("ssq_done", "xn_ready", "xt_filled", "x_ready", "h_ready"))
    o_filled, o_ready = sem("o_filled"), sem("o_ready")
    out_done = sem("out_done")

    cv3 = lambda t: t.rearrange("p (a b) -> p a b", a=KC)

    def bc(ap, axis, shape):
        return ap.unsqueeze(axis).broadcast_to(shape)

    chains = {}
    signalled = {}

    def signal(which, ins, s):
        signalled[s.name] = signalled.get(s.name, 0) + 1
        ins.then_inc(s, 1)
        chains[which].eng.wait_ge(s, signalled[s.name])

    def sig_a(ins, s):
        signal("a", ins, s)

    def sig_v(ins, s):
        signal("v", ins, s)

    def unit_wait(pe, u):
        pe.wait_ge(hi_done, u + 1)
        pe.wait_ge(lo_done, u + 1)

    def three(pe, o, ah, al, bh, bl, start, stop):
        pe.matmul(o, ah, bh, start=start, stop=False)
        pe.matmul(o, ah, bl, start=False, stop=False)
        return pe.matmul(o, al, bh, start=False, stop=stop)

    def pe_a(pe, s, outs, c0=META, n=SEQ):
        wh, wl = cv3(hi[s][:]), cv3(lo[s][:])
        for f in range(2):
            for k in range(KC):
                m = three(pe, outs[f], wh[:, k, f * P:(f + 1) * P], wl[:, k, f * P:(f + 1) * P],
                          xh[:, k, c0:c0 + n], xl[:, k, c0:c0 + n], k == 0, k == KC - 1)
        m.then_inc(unit_used, 1)

    def pe_b(pe, s, outs, width=256):
        wh, wl = cv3(hi[s][:]), cv3(lo[s][:])
        for o, c, m_ in outs:
            for k in range(KC):
                m = three(pe, o, xh[:, k, c:c + m_], xl[:, k, c:c + m_], wh[:, k, 0:width], wl[:, k, 0:width],
                          k == 0, k == KC - 1)
        m.then_inc(unit_used, 1)

    def pe_v(pe, s, ah, al, first_k, last_k):
        wh = hi[s][:].rearrange("p (a b) -> p a b", a=2)
        wl = lo[s][:].rearrange("p (a b) -> p a b", a=2)
        for kk in range(2):
            for t in range(NT):
                for n in range(2):
                    m = three(pe, ps[:, 4 + 2 * t + n, :], ah[:, kk, t * P:(t + 1) * P], al[:, kk, t * P:(t + 1) * P],
                              wh[:, kk, n * 512:(n + 1) * 512], wl[:, kk, n * 512:(n + 1) * 512],
                              first_k and kk == 0, last_k and kk == 1)
        m.then_inc(unit_used, 1)

    XT = ((0, 0), (0, 1), (1, 0), (1, 1))
    norm_fills = [4, 4, 4, 4, 5, 4]

    def pe_norm(pe, k):
        pe.wait_ge(xn_ready, k + 1)
        before = sum(norm_fills[:k])
        fills = list(XT) + ([None] if norm_fills[k] == 5 else [])
        for q, fill in enumerate(fills):
            if q >= 2:
                pe.wait_ge(x_ready, before + q - 1)
            b = 2 + q % 2
            if fill is None:
                for c in range(KC):
                    m = pe.transpose(ps[:, b, c * META:(c + 1) * META], hm[:, c * P:(c + 1) * P], ident[0:META, 0:META])
            else:
                t, half = fill
                for c in range(4):
                    k_ = half * 4 + c
                    m = pe.transpose(ps[:, b, c * P:(c + 1) * P], xn[:, t, k_ * P:(k_ + 1) * P], ident[:])
            m.then_inc(xt_filled, 1)
        pe.wait_ge(x_ready, before + len(fills))

    def act_norm(act, k, ready, value):
        act.wait_ge(ready, value)
        for t in range(NT):
            chain_a(nc.scalar.activation(xn[:, t, :], h[:, t, :], ACT.Square,
                                         accum_out=stat[:, t:t + 1]))
        if norm_fills[k] == 5:
            chain_a(nc.scalar.activation(oh_f32[0:META, :], hm[:, :], ACT.Square, accum_out=stat[0:META, 2:3]))
        sig_a(nc.scalar.activation(stat[:, 8:9], stat[:, 0:1], ACT.Copy), ssq_done)

    oh_f32 = sb("oh_f32", [P, D], at=xn_at + 8192)

    def rsqrt(v, chain, dst, src, n):
        m_, w = dst.shape[0], dst.shape[1]
        x, y, t = (rs[0:m_, q, 0:w] for q in range(3))
        chain(v.tensor_scalar(x, src, 1.0 / n, EPS, ALU.mult, ALU.add))
        chain(v.tensor_scalar(y.bitcast(I32), x.bitcast(I32), -0.5, 1597463007.0, ALU.mult, ALU.add))
        for q in range(3):
            chain(v.tensor_tensor(t, y, y, ALU.mult))
            chain(v.scalar_tensor_tensor(t, t, -0.5, x, ALU.mult, ALU.mult))
            chain(v.scalar_tensor_tensor(dst if q == 2 else y, t, 1.5, y, ALU.add, ALU.mult))

    def dve_norm(v, k, gain):
        v.wait_ge(ssq_done, k + 1)
        rsqrt(v, chain_v, stat[:, 4:6], stat[:, 0:2], D)
        for t in range(NT):
            chain_v(v.tensor_scalar(xn[:, t, :], h[:, t, :], stat[:, 4 + t:5 + t], None, ALU.mult))
        if norm_fills[k] == 5:
            rsqrt(v, chain_v, stat[0:META, 6:7], stat[0:META, 2:3], D)
            chain_v(v.tensor_scalar(hm[:, :], hm[:, :], stat[0:META, 6:7], None, ALU.mult))
        chain_mark(v, xn_ready)
        before = sum(norm_fills[:k])
        fills = list(XT) + ([None] if norm_fills[k] == 5 else [])
        for q, fill in enumerate(fills):
            v.wait_ge(xt_filled, before + q + 1)
            b = 2 + q % 2
            if fill is None:
                dh, dl = xh[:, :, 0:META], xl[:, :, 0:META]
                src = ps[:, b, 0:P].rearrange("p (a b) -> p a b", a=KC)
                t32 = tmp[0][:, 0:P].rearrange("p (a b) -> p a b", a=KC)
                g = bc(cols[:, gain:gain + KC], 2, [P, KC, META])
            else:
                t, half = fill
                c0 = META + t * P
                dh = xh[:, half * 4:half * 4 + 4, c0:c0 + P]
                dl = xl[:, half * 4:half * 4 + 4, c0:c0 + P]
                src = ps[:, b, :].rearrange("p (a b) -> p a b", a=4)
                t32 = tmp[0][:].rearrange("p (a b) -> p a b", a=4)
                g = bc(cols[:, gain + half * 4:gain + half * 4 + 4], 2, [P, 4, P])
            chain_v(v.tensor_tensor(t32, src, g, ALU.mult))
            chain_v(v.tensor_copy(dh, t32))
            sig_v(v.tensor_tensor(dl, t32, dh.bitcast(F32), ALU.subtract), x_ready)

    def chain_mark(v, s):
        sig_v(v.memset(stat[:, 127:128], 0.0), s)

    def pe_out(pe, src, nv, u0, done0):
        def fill(n):
            if n >= 2:
                pe.wait_ge(o_ready, done0 + n - 1)
            for kk in range(2):
                for t in range(NT):
                    c = (2 * n + kk) * P
                    m = pe.transpose(ps[:, 2 + n % 2, (kk * 2 + t) * P:(kk * 2 + t + 1) * P], src[:, t, c:c + P], ident[:])
            m.then_inc(o_filled, 1)
        fill(0)
        for n in range(nv):
            if n + 1 < nv:
                fill(n + 1)
            unit_wait(pe, u0 + n)
            pe.wait_ge(o_ready, done0 + n + 1)
            pe_v(pe, (u0 + n) % RING, oh[:, n % 2], ol[:, n % 2], n == 0, n == nv - 1)

    def dve_out(v, nv, gain, u0, done0, value):
        for n in range(nv):
            v.wait_ge(o_filled, done0 + n + 1)
            if n >= 2:
                v.wait_ge(unit_used, u0 + n - 1)
            src = ps[:, 2 + n % 2, :].rearrange("p (a b) -> p a b", a=2)
            t32 = tmp[0][:].rearrange("p (a b) -> p a b", a=2)
            if gain is None:
                chain_v(v.tensor_copy(t32, src))
            else:
                chain_v(v.tensor_tensor(t32, src, bc(cols[:, gain + 2 * n:gain + 2 * n + 2], 2, [P, 2, SEQ]), ALU.mult))
            chain_v(v.tensor_copy(oh[:, n % 2], t32))
            sig_v(v.tensor_tensor(ol[:, n % 2], t32, oh[:, n % 2].bitcast(F32), ALU.subtract), o_ready)
        dve_residual(v, u0 + nv)

    def dve_residual(v, used):
        v.wait_ge(unit_used, used)
        for t in range(NT):
            for n in range(2):
                hs = h[:, t, n * 512:(n + 1) * 512]
                chain_v(v.tensor_tensor(hs, hs, ps[:, 4 + 2 * t + n, :], ALU.add))
        chain_mark(v, h_ready)

    def split_hi(act, u, slot, rnd):
        act.wait_ge(raw_in[slot], 16 * rnd)
        act.wait_ge(unit_used, u - 2)
        nc.scalar.activation(hi[slot][:], raw[slot][:], ACT.Copy).then_inc(hi_done, 1)

    def act_after(act, u):
        n = u + RING
        if n < U_PEER:
            split_hi(act, n, n % RING, n // RING + 1)

    dt_mm, dt_split, da_ready, acs_mm, acs_ready = (sem(n) for n in ("dt_mm", "dt_split", "da_ready", "acs_mm", "acs_ready"))
    dt_abs, f_abs = sem("dt_abs"), sem("f_abs")
    dt_e, dt_ln, da_exp, acs_e = (sem(n) for n in ("dt_e", "dt_ln", "da_exp", "acs_e"))
    xbc_conv, xbc_silu, xs_filled, xs_evac, bt_filled = (sem(n) for n in ("xbc_conv", "xbc_silu", "xs_filled", "xs_evac", "bt_filled"))
    cb_mm, cb_ready, row_mm, row_min, dec_ready, m_ready, y_mm, yoff_mm = (
        sem(n) for n in ("cb_mm", "cb_ready", "row_mm", "row_min", "dec_ready", "m_ready", "y_mm", "yoff_mm"))
    xdst_ready, st_mm, st_ready, z_evac, y_added, gated, g_ssq, y_ready = (
        sem(n) for n in ("xdst_ready", "st_mm", "st_ready", "z_evac", "y_added", "gated", "g_ssq", "y_ready"))
    f_conv, f_silu, f_read, f_hid, f_chain = (sem(n) for n in ("f_conv", "f_silu", "f_read", "f_hid", "f_chain"))
    wf_loaded, wf_split, f_mm, f_e, f_l, f_s, cum_in, cum_mm = (sem(n) for n in (
        "wf_loaded", "wf_split", "f_mm", "f_e", "f_l", "f_s", "cum_in", "cum_mm"))
    b_evac, b_sq, qk_ready = sem("b_evac"), sem("b_sq"), sem("qk_ready")
    t_filled, t_evac, s_mm, s_max, s_exp, pt_filled, pt_evac, o_mm, o_evac, attn_ready = (sem(n) for n in (
        "t_filled", "t_evac", "s_mm", "s_max", "s_exp", "pt_filled", "pt_evac", "o_mm", "o_evac", "attn_ready"))
    meta_loaded, mw_loaded, c_sig, c_read, hc_ready, conv_done = (sem(n) for n in (
        "meta_loaded", "mw_loaded", "c_sig", "c_read", "hc_ready", "conv_done"))
    lat_ssq, lat_n, lat_f, lat_t, uq_mm, uq_evac, ukv_mm, ukv_evac, mqk_ready = (sem(n) for n in (
        "lat_ssq", "lat_n", "lat_f", "lat_t", "uq_mm", "uq_evac", "ukv_mm", "ukv_evac", "mqk_ready"))
    ct_mm, ln_ready, ln_silu, mix_ssq, mix_ready = (sem(n) for n in ("ct_mm", "ln_ready", "ln_silu", "mix_ssq", "mix_ready"))
    keys_z, keys_in, wq_evac, sc_mm, sc_evac, tv_sub, tv_exp, lst_in, lst_mm, lst_out = (sem(n) for n in (
        "keys_z", "keys_in", "wq_evac", "sc_mm", "sc_evac", "tv_sub", "tv_exp", "lst_in", "lst_mm", "lst_out"))
    row_hot, col_hot, col_gates, g_mm, g_evac, a_gelu, w_mul, w_ready, p_chain = (sem(n) for n in (
        "row_hot", "col_hot", "col_gates", "g_mm", "g_evac", "a_gelu", "w_mul", "w_ready", "p_chain"))
    h_saved, h_back, fin_ssq, fin_ready = (sem(n) for n in ("h_saved", "h_back", "fin_ssq", "fin_ready"))
    block_ssq, block_ready = sem("block_ssq"), sem("block_ready")

    block_cm = nc.Block()
    block = block_cm.__enter__()

    @block.sync
    def _(sp):
        def load(slot, src, last):
            if last > 0:
                sp.wait_ge(hi_done, last)
                sp.wait_ge(lo_done, last)
            sp.dma_start(raw[slot][:], src).then_inc(raw_in[slot], 16)

        def run(u0, name, idx):
            for n, i in enumerate(idx):
                u = u0 + n
                load(u % RING, A[name][i], u - 2)

        sp.wait_ge(x_loaded, 16)
        run(U_BC, "w_xbc", range(12))
        run(U_Z, "w_z", range(8))
        run(U_SOUT, "w_sout", range(8))

        def ffn(l, u0):
            run(u0, f"w_up{l}", range(2))
            with nc.sync.Fori(1, FT // 2) as i:
                parts = [(f"w_up{l}", sp.snap(i * 2)), (f"w_down{l}", sp.snap(i - 1)), (f"w_up{l}", sp.snap(i * 2 + 1))]
                split = [sp.snap(i * 3 + (u0 - 3 + n)) for n in range(3)]
                for n, (name, idx) in enumerate(parts):
                    slot = (u0 + 2 + n) % RING
                    src = A[name][bass.ds(idx, 1)].rearrange("o p n -> (o p) n")
                    sp.wait_ge(hi_done, split[n])
                    sp.wait_ge(lo_done, split[n])
                    sp.dma_start(raw[slot][:], src).then_inc(raw_in[slot], 16)
            run(u0 + FFN_UNITS - 1, f"w_down{l}", [FT // 2 - 1])

        ffn(0, U_FFN0)
        run(U_FQ, "w_fox", range(16))
        run(U_FOUT, "w_fout", range(4))
        ffn(1, U_FFN1)
        run(U_CONV, "w_conv", range(4))
        run(U_CQ, "w_lat", range(2))
        run(U_MOUT, "w_mout", range(4))
        run(U_WQ, "w_wq", range(4))
        sp.wait_ge(hi_done, U_PEER - 1)
        sp.wait_ge(lo_done, U_PEER - 1)
        sp.dma_start(raw[0][:], A["w_u"][0]).then_inc(raw_in[0], 16)
        sp.wait_ge(hi_u_done, 1)
        sp.wait_ge(lo_u_done, 1)
        sp.dma_start(raw[0][:], A["w_u"][1]).then_inc(raw_in[0], 16)
        sp.wait_ge(g_mm, 2 * GROUPS_OF_TOKENS)
        sp.dma_start(raw[1][:], A["w_v"][0]).then_inc(raw_in[1], 16)
        with nc.sync.Fori(1, PAIRS - 1) as m:
            sp.wait_ge(hi_u_done, m + 1)
            sp.wait_ge(lo_u_done, m + 1)
            sp.dma_start(raw[0][:], A["w_u"][bass.ds(m + 1, 1)].rearrange("o p n -> (o p) n")).then_inc(raw_in[0], 16)
            sp.wait_ge(hi_v_done, m)
            sp.wait_ge(lo_v_done, m)
            sp.dma_start(raw[1][:], A["w_v"][bass.ds(m, 1)].rearrange("o p n -> (o p) n")).then_inc(raw_in[1], 16)
        sp.wait_ge(hi_v_done, PAIRS - 1)
        sp.wait_ge(lo_v_done, PAIRS - 1)
        sp.dma_start(raw[1][:], A["w_v"][PAIRS - 1]).then_inc(raw_in[1], 16)
        sp.wait_ge(w_mul, 32)
        sp.wait_ge(h_saved, 16)
        sp.dma_start(hf[:].rearrange("p a b -> p (a b)"), h_save).then_inc(h_back, 16)
        sp.dma_start(gfin[:], A["gfin"][0].partition_broadcast(P)).then_inc(h_back, 16)
        sp.wait_ge(fin_ready, 1)
        sp.dma_start(out[0].rearrange("(t p) d -> p t d", p=P), fo[:]).then_inc(out_done, 16)
        sp.wait_ge(out_done, 16)

    @block.gpsimd
    def _(pool):
        g = nc.gpsimd
        chain = Chain(pool, pool_c)
        chain(g.memset(ident[:], 0.0))
        chain(g.affine_select(ident[:], ident[:], [[-1, P]], ALU.not_equal, 1.0, base=0, channel_multiplier=1))
        chain(g.memset(ones[:], 1.0))
        chain(g.affine_select(tri[:], ones[:], [[1, P]], ALU.is_ge, 0.0, base=0, channel_multiplier=-1))
        chain(g.tensor_copy(identb[:], ident[:]))
        chain(g.memset(negm[:], 0.0))
        chain(g.affine_select(negm[:, T2 - P:], negm[:, T2 - P:], [[-1, P]], ALU.is_ge, -1e30, base=0, channel_multiplier=1))
        g.iota(iota[:], [[1, P]], base=0, channel_multiplier=0, allow_small_or_imprecise_dtypes=True).then_inc(consts, 1)

        def second(slot):
            return g.tensor_tensor(lo[slot][:], raw[slot][:], hi[slot][:].bitcast(F32), ALU.subtract)

        for u in range(RING):
            pool.wait_ge(hi_done, u + 1)
            second(u).then_inc(lo_done, 1)
        full = (U_PEER - RING) // RING
        with nc.gpsimd.Fori(0, full) as i:
            for s in range(RING):
                pool.wait_ge(hi_done, i * RING + (RING + s + 1))
                second(s).then_inc(lo_done, 1)
        for u in range(RING * (full + 1), U_PEER):
            pool.wait_ge(hi_done, u + 1)
            second(u % RING).then_inc(lo_done, 1)
        def weigh_columns(n, b):
            pool.wait_ge(col_hot, n + 1)
            gate = lst[:, 2, bass.ds(n * GT, GT)].unsqueeze(2).broadcast_to([P, GT, P])
            g.tensor_tensor(oj[b][:], oj[b][:], gate, ALU.mult).then_inc(col_gates, 1)

        for n in range(2):
            weigh_columns(n, n)
        with nc.gpsimd.Fori(0, (GROUPS_OF_TOKENS - 2) // 3) as i:
            for k in range(3):
                weigh_columns(i * 3 + (2 + k), (2 + k) % 3)

    def chain_a(ins):
        chains["a"](ins)

    def chain_v(ins):
        chains["v"](ins)

    CORE = [(g, c) for g in range(GROUPS) for c in range(NT)]
    ATT = {"fox": (FH, 0), "mla": (MH, FH)}

    @block.tensor
    def _(pe):
        def dt_rows():
            pe.wait_ge(dt_split, 1)
            for t in range(NT):
                for k in range(KC):
                    c = META + t * P
                    m = three(pe, ps[:, 4, t * HEADS:(t + 1) * HEADS], xh[:, k, c:c + P], xl[:, k, c:c + P],
                              wdth[:, k, :], wdtl[:, k, :], k == 0, k == KC - 1)
            m.then_inc(dt_mm, 1)

        def cumsum():
            pe.wait_ge(da_ready, 1)
            for c in range(NT):
                pe.matmul(ps[:, 5, c * HEADS:(c + 1) * HEADS], tri[:], dtv[:, 1, c, :], start=True, stop=True)
            pe.matmul(ps[:, 5, 2 * HEADS:3 * HEADS], ones[:], dtv[:, 1, 0, :], start=True, stop=True).then_inc(acs_mm, 1)

        def xs_turn(v):
            pe.wait_ge(xbc_silu, 4 + v + 1)
            pe.wait_ge(xs_evac, max(v, 1))
            for c in range(NT):
                for f in range(2):
                    m = pe.transpose(ps[:, 2 + v % 2, (c * 2 + f) * P:(c * 2 + f + 1) * P],
                                     xsf[v % 2][:, f, c * P:(c + 1) * P], ident[:])
            m.then_inc(xs_filled, 1)

        def ssd():
            pe.wait_ge(consts, 1)
            pe_norm(pe, 0)
            dt_rows()
            for u in range(12):
                unit_wait(pe, u)
                if u >= 2:
                    pe.wait_ge(xbc_conv, u - 1)
                pe_a(pe, u % RING, [ps[:, u % 2, 0:SEQ], ps[:, u % 2, SEQ:2 * SEQ]])
                if u == 1:
                    cumsum()
                if u == 3:
                    pe.wait_ge(xbc_silu, 2)
                    for g in range(GROUPS):
                        m = pe.transpose(ps[:, 2, g * P:(g + 1) * P], bct[:, g, 0:P], ident[:])
                    m.then_inc(bt_filled, 1)
                if u >= 5:
                    xs_turn(u - 5)
            xs_turn(7)

            def z_unit(n):
                unit_wait(pe, U_Z + n)
                if n < 2:
                    pe.wait_ge(xbc_conv, 12)
                else:
                    pe.wait_ge(z_evac, n - 1)
                pe_b(pe, (U_Z + n) % RING, [(ps[:, n % 2, t * 256:(t + 1) * 256], META + t * P, P) for t in range(NT)])

            def rowbc(i):
                g, c = CORE[i]
                pe.wait_ge(acs_ready, 1)
                if i >= 1:
                    pe.wait_ge(row_min, i)
                for r in range(HPG):
                    hd = g * HPG + r
                    m = pe.matmul(ps[:, 4 + r // 4, (r % 4) * P:(r % 4 + 1) * P],
                                  dtv[:, 1, c, hd:hd + 1].broadcast_to([P, P]), tri[:], start=True, stop=True)
                m.then_inc(row_mm, 1)

            def y_diag(i):
                pe.wait_ge(m_ready, i + 1)
                if i >= 1:
                    pe.wait_ge(y_added, i)
                for r in range(HPG):
                    m = pe.matmul(ps[:, 6, r * HD:(r + 1) * HD], dec[i % 2][:, r, :], xdt[i % 2][:, r, :], start=True, stop=True)
                m.then_inc(y_mm, 1)
                g, c = CORE[i]
                if c == 1:
                    pe.wait_ge(st_ready, g + 1)
                    pe.matmul(ps[:, 7, :], bct[:, GROUPS + g, P:2 * P], st_t[:], start=True, stop=True).then_inc(yoff_mm, 1)

            for g in range(GROUPS):
                if g == 0:
                    pe.wait_ge(xs_evac, 9)
                    pe.wait_ge(xbc_silu, 12)
                else:
                    pe.wait_ge(cb_ready, g)
                for c in range(NT):
                    m = pe.matmul(ps[:, 2, c * P:(c + 1) * P], bct[:, g, c * P:(c + 1) * P],
                                  bct[:, GROUPS + g, c * P:(c + 1) * P], start=True, stop=True)
                m.then_inc(cb_mm, 1)
                for i in (2 * g, 2 * g + 1):
                    rowbc(i)
                    if i >= 1:
                        y_diag(i - 1)
                    z_unit(i)
                    if i == 2 * g:
                        pe.wait_ge(xdst_ready, g + 1)
                        if g >= 1:
                            pe.wait_ge(st_ready, g)
                        pe.matmul(ps[:, 3, :], b_tm[:, g, :], xdst[:].rearrange("p a b -> p (a b)"),
                                  start=True, stop=True).then_inc(st_mm, 1)
            y_diag(7)
            pe.wait_ge(y_ready, 1)
            pe_out(pe, y_tm, 8, U_SOUT, 0)

        def ffn(l, u0):
            b = l * FT
            pe_norm(pe, 1 + 2 * l)

            def up(j, u, par, slot):
                pe.wait_ge(hi_done, u + 1)
                pe.wait_ge(lo_done, u + 1)
                if not isinstance(j, int) or j >= 2:
                    pe.wait_ge(f_read, j + (b - 1))
                pe_a(pe, slot, [ps[:, par, 0:SEQ], ps[:, par, SEQ:2 * SEQ]])

            def down(n, u, slot, first_k, last_k):
                pe.wait_ge(hi_done, u + 1)
                pe.wait_ge(lo_done, u + 1)
                pe.wait_ge(f_hid, n * 2 + (b + 2))
                pe_v(pe, slot, hdh, hdl, first_k, last_k)

            up(0, u0, 0, u0 % RING)
            up(1, u0 + 1, 1, (u0 + 1) % RING)
            up(2, u0 + 2, 0, (u0 + 2) % RING)
            down(0, u0 + 3, u0 % RING, True, False)
            up(3, u0 + 4, 1, (u0 + 4) % RING)
            with nc.tensor.Fori(2, FT // 2) as i:
                up(i * 2, i * 3 + (u0 - 1), 0, (u0 + 2) % RING)
                down(i - 1, i * 3 + u0, u0 % RING, False, False)
                up(i * 2 + 1, i * 3 + (u0 + 1), 1, (u0 + 1) % RING)
            down(FT // 2 - 1, u0 + FFN_UNITS - 1, (u0 + FFN_UNITS - 1) % RING, False, True)

        def attention(kind):
            H, h0 = ATT[kind]
            mla = kind == "mla"
            dq = QD if mla else DA

            def turn(n):
                pe.wait_ge(t_evac, h0 + n) if n >= 1 else None
                if mla:
                    for t in range(NT):
                        pe.transpose(ps[0:dq, 0, t * P:(t + 1) * P], mq[:, t, n, :], ident[:])
                    pe.transpose(ps[0:dq, 0, 2 * P:2 * P + META], mk[0:META, 0, n, :], ident[0:META, 0:META])
                    for t in range(NT):
                        m = pe.transpose(ps[0:dq, 1, t * P:(t + 1) * P], mk[:, 1 + t, n, :], ident[:])
                else:
                    for t in range(NT):
                        pe.transpose(ps[0:dq, n % 2, t * P:(t + 1) * P], fq[:, t, n, :], ident[:])
                    for t in range(NT):
                        m = pe.transpose(ps[0:dq, n % 2, (2 + t) * P:(3 + t) * P], fk[:, t, n, :], ident[:])
                m.then_inc(t_filled, 1)

            def scores(n):
                pe.wait_ge(t_evac, h0 + n + 1)
                if n >= 1:
                    pe.wait_ge(s_exp, h0 + n)
                    if n >= 2:
                        pe.wait_ge(s_exp, h0 + n - 1)
                b = 2 + n % 2
                if mla:
                    qt = mqt[0]
                    k0 = SEQ
                    n0, n1 = META + P, META + 2 * P
                else:
                    qt = qkt[n % 2][:].rearrange("p a b -> p (a b)")
                    k0 = SEQ
                    n0, n1 = P, 2 * P
                pe.matmul(ps[:, b, 0:n0], qt[0:dq, 0:P], qt[0:dq, k0:k0 + n0], start=True, stop=False)
                pe.matmul(ps[:, b, 0:n0], identb[:], negm[:, T2 - n0:], start=False, stop=True)
                pe.matmul(ps[:, b, n0:n0 + n1], qt[0:dq, P:2 * P], qt[0:dq, k0:k0 + n1], start=True, stop=False)
                pe.matmul(ps[:, b, n0:n0 + n1], identb[:], negm[:, T2 - n1:], start=False, stop=True).then_inc(s_mm, 1)

            def turn_p(n):
                pe.wait_ge(s_exp, h0 + n + 1)
                if n >= 1:
                    pe.wait_ge(pt_evac, h0 + n)
                if mla:
                    pm = mp[0]
                    for i, c in enumerate((META, META + P + META, META + P + META + P)):
                        pe.transpose(ps[:, 4, i * P:(i + 1) * P], pm[:, c:c + P], ident[:])
                    for i, c in enumerate((0, META + P)):
                        m = pe.transpose(ps[0:META, 5, i * P:(i + 1) * P], pm[:, c:c + META], ident[:])
                else:
                    for i in range(3):
                        m = pe.transpose(ps[:, 4, i * P:(i + 1) * P], pr[n % 2][:, i, :], ident[:])
                m.then_inc(pt_filled, 1)

            def values(n):
                pe.wait_ge(pt_evac, h0 + n + 1)
                b = 6 + (n // 4) % 2
                if n % 4 == 0 and n >= 8:
                    pe.wait_ge(o_evac, h0 // 4 + n // 4 - 1)
                r = n % 4
                o = [ps[:, b, (t * 4 + r) * HD:(t * 4 + r + 1) * HD] for t in range(NT)]
                if mla:
                    pt = mpt[0]
                    val = lambda t: mv[:, 1 + t, n, :]
                    vm = mv[0:META, 0, n, :]
                    pe.matmul(o[0], pt[0:META, 3, :], vm, start=True, stop=False)
                    pe.matmul(o[0], pt[:, 0, :], val(0), start=False, stop=True)
                    pe.matmul(o[1], pt[0:META, 4, :], vm, start=True, stop=False)
                    pe.matmul(o[1], pt[:, 1, :], val(0), start=False, stop=False)
                    pe.matmul(o[1], pt[:, 2, :], val(1), start=False, stop=True).then_inc(o_mm, 1)
                else:
                    pt = prt[n % 2]
                    val = lambda t: fv[:, t, n * HD:(n + 1) * HD]
                    pe.matmul(o[0], pt[:, 0, :], val(0), start=True, stop=True)
                    pe.matmul(o[1], pt[:, 1, :], val(0), start=True, stop=False)
                    pe.matmul(o[1], pt[:, 2, :], val(1), start=False, stop=True).then_inc(o_mm, 1)

            turn(0)
            for n in range(H):
                scores(n)
                if n + 1 < H:
                    turn(n + 1) if not mla else None
                if n >= 1 and not mla:
                    values(n - 1)
                turn_p(n)
                if mla:
                    if n + 1 < H:
                        turn(n + 1)
                    values(n)
            if not mla:
                values(H - 1)

        def fox():
            pe_norm(pe, 2)
            pe.wait_ge(wf_split, 1)
            for t in range(NT):
                for k in range(KC):
                    c = META + t * P
                    m = three(pe, ps[:, 4, t * FH:(t + 1) * FH], xh[:, k, c:c + P], xl[:, k, c:c + P],
                              wfh[:, k, :], wfl[:, k, :], k == 0, k == KC - 1)
            m.then_inc(f_mm, 1)
            for n in range(16):
                unit_wait(pe, U_FQ + n)
                if n >= 2:
                    pe.wait_ge(b_evac, n - 1)
                pe_b(pe, (U_FQ + n) % RING, [(ps[:, n % 2, t * 256:(t + 1) * 256], META + t * P, P) for t in range(NT)])
                if n == 2:
                    pe.wait_ge(cum_in, 1)
                    pe.matmul(ps[:, 5, 0:FH], tri[:], fst[:, 2, 0, :], start=True, stop=True)
                    pe.matmul(ps[:, 5, FH:2 * FH], ones[:], fst[:, 2, 0, :], start=True, stop=False)
                    pe.matmul(ps[:, 5, FH:2 * FH], tri[:], fst[:, 2, 1, :], start=False, stop=True).then_inc(cum_mm, 1)
            pe.wait_ge(b_evac, 16)
            pe.wait_ge(qk_ready, 1)
            attention("fox")
            pe.wait_ge(attn_ready, 1)
            pe_out(pe, xn, 4, U_FOUT, 8)

        def mla():
            pe_norm(pe, 4)
            for n in range(4):
                unit_wait(pe, U_CONV + n)
                if n >= 2:
                    pe.wait_ge(c_read, n - 1)
                b = 4 * (n % 2)
                pe_a(pe, (U_CONV + n) % RING, [ps[:, b, 0:T2], ps[:, b + 1, 0:T2]], c0=0, n=T2)
            unit_wait(pe, U_CQ)
            pe_b(pe, U_CQ % RING, [(ps[:, 6, t * 256:(t + 1) * 256], META + t * P, P) for t in range(NT)])
            unit_wait(pe, U_CKV)
            pe_b(pe, U_CKV % RING, [(ps[0:META, 7, 0:160], 0, META)] +
                 [(ps[:, 7, (1 + t) * 160:(2 + t) * 160], META + t * P, P) for t in range(NT)], width=160)
            pe.wait_ge(lat_n, 1)
            for k in range(2):
                for t in range(NT):
                    m = pe.transpose(ps[:, 2, (k * 2 + t) * P:(k * 2 + t + 1) * P], tmp[1][:, t * 256 + k * P:t * 256 + (k + 1) * P], ident[:])
            m.then_inc(lat_f, 1)
            pe.wait_ge(lat_n, 2)
            pe.transpose(ps[:, 3, 0:META], tmp[2][0:META, 0:P], ident[0:META, 0:META])
            for t in range(NT):
                m = pe.transpose(ps[:, 3, META + t * P:META + (t + 1) * P], tmp[2][:, (1 + t) * P:(2 + t) * P], ident[:])
            m.then_inc(lat_f, 1)
            pe.wait_ge(lat_t, 1)
            pe.wait_ge(mw_loaded, 48)
            pe.wait_ge(c_read, 4)
            for t in range(NT):
                for n in range(2):
                    for k in range(2):
                        m = pe.matmul(ps[:, t * 2 + n, 0:384], cqt[:, k, t * P:(t + 1) * P], wuq[:, k, n * 384:(n + 1) * 384],
                                      start=k == 0, stop=k == 1)
                m.then_inc(uq_mm, 1)
                if t == 0:
                    pe.wait_ge(lat_t, 2)
            toks = [(0, META), (META, P), (META + P, P)]
            for i, (c, m_) in enumerate(toks):
                b0 = 4 + 2 * (i % 2)
                if i == 2:
                    pe.wait_ge(ukv_evac, 1)
                for n in range(2):
                    m = pe.matmul(ps[0:m_, b0 + n, :], ckt[:, c:c + m_], wukv[:, n * 512:(n + 1) * 512], start=True, stop=True)
                m.then_inc(ukv_mm, 1)
            pe.wait_ge(mqk_ready, 1)
            attention("mla")
            pe.wait_ge(conv_done, 1)
            for t in range(NT):
                for c in range(CT):
                    m = pe.transpose(ps[:, t, c * P:(c + 1) * P], ca[:, c, t * P:(t + 1) * P], ident[:])
            m.then_inc(ct_mm, 1)
            pe.wait_ge(mix_ready, 1)
            pe_out(pe, mix, 4, U_MOUT, 12)

        def routing():
            pe_norm(pe, 5)
            for n in range(4):
                unit_wait(pe, U_WQ + n)
                if n >= 2:
                    pe.wait_ge(wq_evac, n - 1)
                pe_a(pe, (U_WQ + n) % RING, [ps[:, n % 2, 0:SEQ], ps[:, n % 2, SEQ:2 * SEQ]])
            pe.wait_ge(wq_evac, 4)
            pe.wait_ge(keys_in, 32)
            for n in range(NT * PH // 2):
                t, q = n // 4, n % 4
                if n >= 2:
                    pe.wait_ge(sc_evac, n - 1)
                for r in range(2):
                    hd = 2 * q + r
                    m = pe.matmul(ps[:, 2 + n % 2, r * 256:(r + 1) * 256], qp[:, hd, t * P:(t + 1) * P], keys[:, hd, :],
                                  start=True, stop=True)
                m.then_inc(sc_mm, 1)
            pe.wait_ge(lst_in, 1)
            for w, src in enumerate((sif_sel[0], sif_sel[1], tv)):
                for t in range(NT):
                    m = pe.transpose(ps[:, w, t * P:(t + 1) * P], src[:, t].rearrange("p a b -> p (a b)"), ident[:])
            m.then_inc(lst_mm, 1)

        def experts():
            pe.wait_ge(lst_out, 1)
            def gate_products(b, half):
                for t in range(4):
                    m = pe.matmul(ps[:, 2 * b + half, t * P:(t + 1) * P], oi[b][:, half * 4 + t, :], oj[b][:, half * 4 + t, :],
                                  start=True, stop=True)
                m.then_inc(g_mm, 1)

            for n in range(3):
                pe.wait_ge(row_hot, n + 1)
                pe.wait_ge(col_gates, n + 1)
                for half in range(2):
                    gate_products(n, half)
            for n in range(3, 5):
                pe.wait_ge(row_hot, n + 1)
                pe.wait_ge(col_gates, n + 1)
                for half in range(2):
                    pe.wait_ge(g_evac, 2 * n + half - 5)
                    gate_products(n % 3, half)
            with nc.tensor.Fori(0, (GROUPS_OF_TOKENS - 5) // 3) as i:
                for k in range(3):
                    pe.wait_ge(row_hot, i * 3 + (6 + k))
                    pe.wait_ge(col_gates, i * 3 + (6 + k))
                    for half in range(2):
                        pe.wait_ge(g_evac, i * 6 + (2 * (5 + k) + half - 5))
                        gate_products((5 + k) % 3, half)

            def u_unit(m, gelus):
                pe.wait_ge(hi_u_done, m + 1)
                pe.wait_ge(lo_u_done, m + 1)
                if gelus:
                    pe.wait_ge(a_gelu, m)
                pe_a(pe, 0, [ps[:, 0, 0:SEQ], ps[:, 0, SEQ:2 * SEQ]])

            def v_unit(m, first_k, last_k):
                pe.wait_ge(hi_v_done, m + 1)
                pe.wait_ge(lo_v_done, m + 1)
                pe.wait_ge(w_ready, m + 1)
                pe_v(pe, 1, wgh, wgl, first_k, last_k)

            pe.wait_ge(g_evac, SEQ // 4)
            u_unit(0, False)
            u_unit(1, True)
            v_unit(0, True, False)
            with nc.tensor.Fori(1, PAIRS - 1) as m:
                u_unit(m + 1, True)
                v_unit(m, False, False)
            v_unit(PAIRS - 1, False, True)

        ssd()
        ffn(0, U_FFN0)
        fox()
        ffn(1, U_FFN1)
        mla()
        routing()
        experts()

    @block.scalar
    def _(act):
        chains["a"] = Chain(act, act_c)
        s = nc.scalar
        act.dma_start(h[:], A["x"][0].rearrange("(t p) d -> p t d", p=P)).then_inc(x_loaded, 16)
        act.dma_start(cols[:], A["cols"]).then_inc(cols_loaded, 16)
        act.dma_start(rows[:], A["rows"][0].partition_broadcast(P)).then_inc(rows_loaded, 16)
        act.dma_start(wdt[:], A["w_dt"]).then_inc(wdt_loaded, 16)
        act_norm(act, 0, x_loaded, 16)
        for u in range(RING):
            act.wait_ge(raw_in[u], 16)
            s.activation(hi[u][:], raw[u][:], ACT.Copy).then_inc(hi_done, 1)

        def softplus_neg(e, l, src, ready, n, e_sem, l_sem):
            act.wait_ge(ready, n)
            sig_a(s.activation(e, src, ACT.Exp, scale=-1.0), e_sem)
            act.wait_ge(e_sem, 1)
            sig_a(s.activation(l, e, ACT.Ln, bias=1.0), l_sem)

        def ssd():
            def xs_out(v):
                act.wait_ge(xs_filled, v + 1)
                sig_a(s.activation(x_tm[:, :, v * 256:(v + 1) * 256],
                             ps[:, 2 + v % 2, :].rearrange("p (a b) -> p a b", a=2), ACT.Copy), xs_evac)
            for u in range(12):
                if u == 1:
                    softplus_neg(dtv[:, 2], dtv[:, 3], dtv[:, 4], dt_abs, 1, dt_e, dt_ln)
                    act.wait_ge(rows_loaded, 16)
                    sig_a(s.activation(dtv[:, 5, 0, :], rows[:, ROWS["alog"]:ROWS["alog"] + HEADS], ACT.Exp), da_exp)
                if u == 3:
                    act.wait_ge(acs_ready, 1)
                    s.activation(dtv[:, 8, 0, :], dtv[:, 7, 0, :], ACT.Exp)
                    sig_a(s.activation(dtv[:, 9], dtv[:, 6], ACT.Exp), acs_e)
                act.wait_ge(xbc_conv, u + 1)
                if u < 4:
                    dst = bct[:, 2 * u:2 * u + 2, :]
                else:
                    v = u - 4
                    if v >= 2:
                        act.wait_ge(xs_filled, v - 1)
                    dst = xsf[v % 2][:]
                sig_a(s.activation(dst, cv[u % 2][:], ACT.Silu), xbc_silu)
                act_after(act, u)
                if u == 4:
                    act.wait_ge(bt_filled, 1)
                    sig_a(s.activation(b_tm[:].rearrange("p a b -> p (a b)"), ps[:, 2, :], ACT.Copy), xs_evac)
                if u >= 5:
                    xs_out(u - 5)
            xs_out(7)

            def z_out(n):
                g = n // 2
                act.wait_ge(unit_used, U_Z + n + 1)
                if g >= 1 and n % 2 == 0:
                    act.wait_ge(gated, 2 * g)
                src = ps[:, n % 2, :].rearrange("p (a b) -> p a b", a=2)
                for t in range(NT):
                    ins = s.activation(sz[t][:, (n % 2) * 256:(n % 2 + 1) * 256], src[:, t, :], ACT.Silu)
                sig_a(ins, z_evac)
                act_after(act, U_Z + n)

            def squares(i):
                g, c = CORE[i]
                act.wait_ge(gated, i + 1)
                sig_a(s.activation(xdst_sq[:], y_tm[:, c, g * 512:(g + 1) * 512], ACT.Square,
                             accum_out=stat[:, 16 + i:17 + i]), g_ssq)

            def exps(i):
                act.wait_ge(row_min, i + 1)
                sig_a(s.activation(dec[i % 2][:], dec[i % 2][:], ACT.Exp), dec_ready)

            for g in range(GROUPS):
                exps(2 * g)
                act.wait_ge(st_mm, g + 1)
                if g >= 1:
                    act.wait_ge(yoff_mm, g)
                sig_a(s.activation(st_t[:], ps[:, 3, :], ACT.Copy), st_ready)
                if g >= 1:
                    squares(2 * g - 2)
                    squares(2 * g - 1)
                exps(2 * g + 1)
                z_out(2 * g)
                z_out(2 * g + 1)
            squares(6)
            squares(7)
            for n in range(8):
                act.wait_ge(unit_used, U_SOUT + n + 1)
                act_after(act, U_SOUT + n)

        xdst_sq = cbm_sq

        def ffn(l, u0):
            act_norm(act, 1 + 2 * l, h_ready, 1 + 2 * l)
            b = l * FT

            def silu(j):
                act.wait_ge(f_conv, j + (b + 1))
                s.activation(fcv[:], fcv[:], ACT.Silu).then_inc(f_silu, 1)

            def after(u, slot, rnd):
                act.wait_ge(raw_in[slot], rnd * 16)
                act.wait_ge(unit_used, u - (RING - 1))
                s.activation(hi[slot][:], raw[slot][:], ACT.Copy).then_inc(hi_done, 1)

            silu(0)
            act_after(act, u0)
            silu(1)
            act_after(act, u0 + 1)
            with nc.scalar.Fori(1, FT // 2) as i:
                silu(i * 2)
                n = u0 + 2
                after(i * 3 + n, n % RING, i + (n // RING + 1))
                n = u0 + 3
                after(i * 3 + n, n % RING, i + (n // RING + 1))
                silu(i * 2 + 1)
                n = u0 + 4
                after(i * 3 + n, n % RING, i + (n // RING + 1))
            act.wait_ge(unit_used, u0 + FFN_UNITS)
            act_after(act, u0 + FFN_UNITS - 1)

        def attention(kind):
            H, h0 = ATT[kind]
            mla = kind == "mla"
            dq = QD if mla else DA

            def turned(n):
                act.wait_ge(t_filled, h0 + n + 1)
                if n >= 1:
                    act.wait_ge(s_mm, h0 + n) if mla else (act.wait_ge(s_mm, h0 + n - 1) if n >= 2 else None)
                if mla:
                    s.activation(mqt[0][0:dq, 0:SEQ + META], ps[0:dq, 0, 0:SEQ + META], ACT.Copy)
                    sig_a(s.activation(mqt[0][0:dq, SEQ + META:], ps[0:dq, 1, 0:SEQ], ACT.Copy), t_evac)
                else:
                    sig_a(s.activation(qkt[n % 2][0:dq].rearrange("p a b -> p (a b)"), ps[0:dq, n % 2, :], ACT.Copy), t_evac)

            def exps(n):
                act.wait_ge(s_max, h0 + n + 1)
                b = 2 + n % 2
                if mla:
                    pm, n0, n1 = mp[0], META + P, META + 2 * P
                    if n >= 1:
                        act.wait_ge(pt_filled, h0 + n)
                    st = mst
                else:
                    pm, n0, n1 = pr[n % 2][:].rearrange("p a b -> p (a b)"), P, 2 * P
                    if n >= 2:
                        act.wait_ge(pt_filled, h0 + n - 1)
                    st = stat[:, 32:32 + 96]
                mx, sm = st[:, 2 * (n % 4):2 * (n % 4) + 2], st[:, 16 + 2 * n:16 + 2 * n + 2]
                s.activation(pm[:, 0:n0], ps[:, b, 0:n0], ACT.Exp, bias=mx[:, 0:1], accum_out=sm[:, 0:1])
                sig_a(s.activation(pm[:, n0:n0 + n1], ps[:, b, n0:n0 + n1], ACT.Exp, bias=mx[:, 1:2],
                             accum_out=sm[:, 1:2]), s_exp)

            turned(0)
            for n in range(H):
                if not mla and n + 1 < H:
                    turned(n + 1)
                exps(n)
                if mla and n + 1 < H:
                    turned(n + 1)

        def fox():
            act.wait_ge(h_ready, 2)
            act.dma_start(wf[:], A["w_f"]).then_inc(wf_loaded, 16)
            act_norm(act, 2, h_ready, 2)
            softplus_neg(fst[:, 3], fst[:, 4], fst[:, 5], f_abs, 1, f_e, f_l)
            for n in range(16):
                act.wait_ge(unit_used, U_FQ + n + 1)
                src = ps[:, n % 2, :].rearrange("p (a b) -> p a b", a=2)
                kind, part = n // 4, n % 4
                sl = slice(part * 256, (part + 1) * 256)
                if kind < 2:
                    dst = (fq, fk)[kind]
                    for t in range(NT):
                        s.activation(dst[:, t, 4 * part:4 * part + 4, 0:HD],
                                     src[:, t, :].rearrange("p (a b) -> p a b", a=4), ACT.Copy)
                    if n >= 1:
                        act.wait_ge(b_sq, n)
                    sig_a(s.activation(tmp[1][:], ps[:, n % 2, :], ACT.Square), b_evac)
                elif kind == 2:
                    sig_a(s.activation(fv[:, :, sl], src, ACT.Copy), b_evac)
                else:
                    sig_a(s.activation(fg[:, :, sl], src, ACT.Sigmoid), b_evac)
                act_after(act, U_FQ + n)
            attention("fox")
            for n in range(4):
                act.wait_ge(unit_used, U_FOUT + n + 1)
                act_after(act, U_FOUT + n)

        def mla():
            act.wait_ge(h_ready, 4)
            act.dma_start(hm[:], A["meta"]).then_inc(meta_loaded, 16)
            act.dma_start(wuq[:], A["w_uq"]).then_inc(mw_loaded, 16)
            act.dma_start(wukv[:], A["w_ukv"]).then_inc(mw_loaded, 16)
            act.dma_start(cs[:], A["cs"]).then_inc(mw_loaded, 16)
            for t in range(NT):
                chain_a(s.activation(xn[:, t, :], h[:, t, :], ACT.Square, accum_out=stat[:, t:t + 1]))
            sig_a(s.activation(stat[:, 8:9], stat[:, 0:1], ACT.Copy), block_ssq)
            act.wait_ge(meta_loaded, 16)
            act_norm(act, 4, h_ready, 5)
            for n in range(4):
                act.wait_ge(unit_used, U_CONV + n + 1)
                b = 4 * (n % 2)
                if n >= 1:
                    act.wait_ge(c_read, n)
                sig_a(s.activation(tmp[1][:, 0:T2], ps[:, b + 1, 0:T2], ACT.Sigmoid), c_sig)
                act_after(act, U_CONV + n)
            act.wait_ge(unit_used, U_CQ + 1)
            act.wait_ge(c_read, 4)
            act_after(act, U_CQ)
            for t in range(NT):
                sig_a(s.activation(tmp[3][:, 0:256], ps[:, 6, t * 256:(t + 1) * 256], ACT.Square, accum_out=mst[:, 40 + t:41 + t]), lat_ssq)
                act.wait_ge(lat_ssq, t + 1)
            act.wait_ge(unit_used, U_CKV + 1)
            act_after(act, U_CKV)
            for i in range(3):
                m_ = META if i == 0 else P
                sig_a(s.activation(tmp[3][0:m_, 256:256 + P], ps[0:m_, 7, i * 160:i * 160 + P], ACT.Square,
                             accum_out=mst[0:m_, 42 + i:43 + i]), lat_ssq)
                act.wait_ge(lat_ssq, 3 + i)
            for t in range(NT):
                act.wait_ge(uq_mm, t + 1)
                for n in range(2):
                    ins = s.activation(mq[:, t, 4 * n:4 * n + 4, :], ps[:, t * 2 + n, 0:384].rearrange("p (a b) -> p a b", a=4),
                                       ACT.Copy, scale=1.0 / math.sqrt(QD))
                sig_a(ins, uq_evac)
            for i in range(3):
                m_ = META if i == 0 else P
                act.wait_ge(ukv_mm, i + 1)
                b0 = 4 + 2 * (i % 2)
                for n in range(2):
                    src = ps[0:m_, b0 + n, :].rearrange("p (a b) -> p a b", a=4)
                    s.activation(mk[0:m_, i, 4 * n:4 * n + 4, 0:NOPE], src[:, :, 0:NOPE], ACT.Copy)
                    ins = s.activation(mv[0:m_, i, 4 * n:4 * n + 4, :], src[:, :, NOPE:128], ACT.Copy)
                sig_a(ins, ukv_evac)
            attention("mla")
            for t in range(NT):
                act.wait_ge(ln_ready, t + 1)
                sig_a(s.activation(mix[:, t, 512:1024], mix[:, t, 512:1024], ACT.Silu), ln_silu)
            act.wait_ge(attn_ready, 2)
            act.wait_ge(ln_silu, 2)
            for t in range(NT):
                for half in range(2):
                    chain_a(s.activation(tmp[3][:], mix[:, t, half * 512:(half + 1) * 512], ACT.Square,
                                         accum_out=mst[:, 48 + 2 * t + half:49 + 2 * t + half]))
            sig_a(s.activation(stat[:, 8:9], mst[:, 48:49], ACT.Copy), mix_ssq)
            for n in range(4):
                act.wait_ge(unit_used, U_MOUT + n + 1)
                act_after(act, U_MOUT + n)

        def routing():
            act.wait_ge(h_ready, 6)
            act.dma_start(h_save, h[:].rearrange("p a b -> p (a b)")).then_inc(h_saved, 16)
            act.wait_ge(keys_z, 1)
            act.dma_start(keys[0:64, :, 0:NKEY], A["keys"][0]).then_inc(keys_in, 16)
            act.dma_start(keys[64:128, :, NKEY:2 * NKEY], A["keys"][1]).then_inc(keys_in, 16)
            act_norm(act, 5, h_ready, 6)
            for n in range(4):
                act.wait_ge(unit_used, U_WQ + n + 1)
                sig_a(s.activation(qp[:, 2 * n:2 * n + 2, :].rearrange("p a b -> p (a b)"), ps[:, n % 2, :], ACT.Copy), wq_evac)
                act_after(act, U_WQ + n)
            for n in range(NT * PH // 2):
                t, q = n // 4, n % 4
                act.wait_ge(sc_mm, n + 1)
                sig_a(s.activation(sc[:, t, 4 * q:4 * q + 4, :].rearrange("p a b -> p (a b)"), ps[:, 2 + n % 2, :], ACT.Copy), sc_evac)
            act.wait_ge(raw_in[0], 16 * 44)
            act.wait_ge(unit_used, U_PEER)
            s.activation(hi[0][:], raw[0][:], ACT.Copy).then_inc(hi_u_done, 1)
            act.wait_ge(tv_sub, 1)
            sig_a(s.activation(tv[:], tv[:], ACT.Exp), tv_exp)

        def experts():
            act.wait_ge(lst_out, 1)
            act.wait_ge(h_saved, 16)
            def take_gates(n, half, b):
                act.wait_ge(g_mm, n * 2 + (half + 1))
                s.activation(gates[:, :, bass.ds(n * GT + half * 4, 4)],
                             ps[:, 2 * b + half, :].rearrange("p (t j) -> p j t", t=4), ACT.Copy).then_inc(g_evac, 1)

            for n in range(2):
                for half in range(2):
                    take_gates(n, half, n)
            with nc.scalar.Fori(0, (GROUPS_OF_TOKENS - 2) // 3) as i:
                for k in range(3):
                    for half in range(2):
                        take_gates(i * 3 + (2 + k), half, (2 + k) % 3)

            def gelu(n):
                if n is not None:
                    act.wait_ge(w_ready, n)
                s.activation(gl[:].rearrange("p a b -> p (a b)"), ps[:, 0, :], ACT.Gelu).then_inc(a_gelu, 1)

            def part(slot, rnd):
                act.wait_ge(raw_in[slot], rnd)
                s.activation(hi[slot][:], raw[slot][:], ACT.Copy).then_inc((hi_u_done, hi_v_done)[slot], 1)

            act.wait_ge(unit_used, U_PEER + 1)
            gelu(None)
            part(0, 16 * 45)
            act.wait_ge(g_evac, SEQ // 4)
            part(1, 16 * 44)
            with nc.scalar.Fori(1, PAIRS - 1) as m:
                act.wait_ge(unit_used, m * 2 + U_PEER)
                gelu(m)
                part(0, m * 16 + 16 * 45)
                act.wait_ge(unit_used, m * 2 + (U_PEER + 1))
                part(1, m * 16 + 16 * 44)
            act.wait_ge(unit_used, U_PEER + 2 * (PAIRS - 1))
            gelu(PAIRS - 1)
            act.wait_ge(unit_used, U_PEER + 2 * PAIRS - 1)
            part(1, 16 * (44 + PAIRS - 1))
            for t in range(NT):
                act.wait_ge(h_ready, 7)
                chain_a(s.activation(fo[:, t, :], hf[:, t, :], ACT.Square, accum_out=stat[:, t:t + 1]))
            sig_a(s.activation(stat[:, 8:9], stat[:, 0:1], ACT.Copy), fin_ssq)

        ssd()
        ffn(0, U_FFN0)
        fox()
        ffn(1, U_FFN1)
        mla()
        routing()
        experts()

    @block.vector
    def _(v):
        chains["v"] = Chain(v, dve_c)
        ch = chain_v
        RH = lambda name, n: rows[:, ROWS[name]:ROWS[name] + n]

        def log1p_parts(e, l, d, q):
            ch(v.tensor_scalar(d, e, 1.0, -1.0, ALU.add, ALU.add))
            ch(v.tensor_scalar(q, d, 0.0, None, ALU.is_equal))
            ch(v.tensor_tensor(l, l, q, ALU.add))
            ch(v.tensor_tensor(d, d, q, ALU.add))
            ch(v.reciprocal(d, d))
            ch(v.tensor_tensor(l, l, d, ALU.mult))
            ch(v.tensor_tensor(l, l, e, ALU.mult))

        def ssd():
            v.wait_ge(cols_loaded, 16)
            v.wait_ge(rows_loaded, 16)
            v.wait_ge(wdt_loaded, 16)
            ch(v.tensor_copy(wdth[:], wdt[:]))
            sig_v(v.tensor_tensor(wdtl[:], wdt[:], wdth[:].bitcast(F32), ALU.subtract), dt_split)
            v.wait_ge(consts, 1)
            dve_norm(v, 0, COLS["mix0"])
            v.wait_ge(dt_mm, 1)
            ch(v.tensor_tensor(dtv[:, 10], ps[:, 4, 0:64].rearrange("p (a b) -> p a b", a=2), bc(RH("dtb", HEADS), 1, [P, NT, HEADS]), ALU.add))
            ch(v.tensor_scalar(dtv[:, 11], dtv[:, 10], -1.0, None, ALU.mult))
            sig_v(v.tensor_tensor(dtv[:, 4], dtv[:, 10], dtv[:, 11], ALU.max), dt_abs)

            def dt_finish():
                v.wait_ge(dt_ln, 1)
                log1p_parts(dtv[:, 2], dtv[:, 3], dtv[:, 4], dtv[:, 11])
                ch(v.scalar_tensor_tensor(dtv[:, 0], dtv[:, 10], 0.0, dtv[:, 3], ALU.max, ALU.add))
                v.wait_ge(da_exp, 1)
                ch(v.scalar_tensor_tensor(dtv[:, 1], dtv[:, 0], -1.0, bc(dtv[:, 5, 0, :], 1, [P, NT, HEADS]), ALU.mult, ALU.mult))
                chain_mark(v, da_ready)

            def acs():
                v.wait_ge(acs_mm, 1)
                ch(v.tensor_copy(dtv[:, 6], ps[:, 5, 0:64].rearrange("p (a b) -> p a b", a=2)))
                ch(v.tensor_tensor(dtv[:, 7, 0, :], ps[:, 5, 64:96], dtv[:, 6, 0, :], ALU.subtract))
                chain_mark(v, acs_ready)

            w0 = COLS["sconv"]
            for u in range(12):
                if u == 1:
                    dt_finish()
                if u == 2:
                    acs()
                v.wait_ge(unit_used, u + 1)
                if u >= 2:
                    v.wait_ge(xbc_silu, u - 1)
                tiles = [16 + 2 * u, 17 + 2 * u] if u < 4 else [2 * (u - 4), 2 * (u - 4) + 1]
                for f, tile in enumerate(tiles):
                    src, dst = ps[:, u % 2, f * SEQ:(f + 1) * SEQ], cv[u % 2][:, f, :]
                    w = lambda n: cols[:, w0 + 5 * tile + n:w0 + 5 * tile + n + 1]
                    ch(v.tensor_scalar(dst, src, w(3), w(4), ALU.mult, ALU.add))
                    for s_ in (1, 2, 3):
                        ins = v.scalar_tensor_tensor(dst[:, s_:SEQ], src[:, 0:SEQ - s_], w(3 - s_), dst[:, s_:SEQ], ALU.mult, ALU.add)
                        if s_ < 3 or f == 0:
                            ch(ins)
                sig_v(ins, xbc_conv)
            v.wait_ge(acs_e, 1)
            v.wait_ge(xs_evac, 9)

            def scale_group(g):
                for c in range(NT):
                    i = 2 * g + c
                    v.wait_ge(g_ssq, i + 1)
                    rsqrt(v, ch, stat[:, 24 + i:25 + i], stat[:, 16 + i:17 + i], 512)
                    yg = y_tm[:, c, g * 512:(g + 1) * 512]
                    ch(v.tensor_scalar(yg, yg, stat[:, 24 + i:25 + i], None, ALU.mult))

            hsl = lambda g: slice(g * HPG, (g + 1) * HPG)

            def add_y(i):
                g, c = CORE[i]
                yg = y_tm[:, c, g * 512:(g + 1) * 512]
                v.wait_ge(y_mm, i + 1)
                ch(v.tensor_tensor(yg, yg, ps[:, 6, :], ALU.add))
                if c == 1:
                    v.wait_ge(yoff_mm, g + 1)
                    ch(v.tensor_tensor(tmp[1][:].rearrange("p (a b) -> p a b", a=HPG), ps[:, 7, :].rearrange("p (a b) -> p a b", a=HPG),
                                       bc(dtv[:, 9, 1, hsl(g)], 2, [P, HPG, HD]), ALU.mult))
                    ch(v.tensor_tensor(yg, yg, tmp[1][:], ALU.add))
                chain_mark(v, y_added)

            def gate_group(g):
                v.wait_ge(z_evac, 2 * g + 2)
                for c in range(NT):
                    yg = y_tm[:, c, g * 512:(g + 1) * 512]
                    sig_v(v.tensor_tensor(yg, yg, sz[c][:], ALU.mult), gated)

            for i, (g, c) in enumerate(CORE):
                xg = x_tm[:, c, g * 512:(g + 1) * 512].rearrange("p (a b) -> p a b", a=HPG)
                if c == 0:
                    v.wait_ge(cb_mm, g + 1)
                    ch(v.tensor_tensor(cbm[:], ps[:, 2, 0:256].rearrange("p (a b) -> p a b", a=2), bc(tri[:], 1, [P, NT, P]), ALU.mult))
                    chain_mark(v, cb_ready)
                if i >= 2:
                    v.wait_ge(y_mm, i - 1)
                ch(v.tensor_tensor(xdt[i % 2][:], xg, bc(dtv[:, 0, c, hsl(g)], 2, [P, HPG, HD]), ALU.mult))
                if c == 0:
                    if g >= 1:
                        v.wait_ge(st_mm, g)
                    sig_v(v.tensor_tensor(xdst[:], xdt[i % 2][:], bc(dtv[:, 8, 0, hsl(g)], 2, [P, HPG, HD]), ALU.mult), xdst_ready)
                v.wait_ge(row_mm, i + 1)
                for r in range(HPG):
                    a_s = dtv[:, 6, c, g * HPG + r:g * HPG + r + 1]
                    ins = v.tensor_scalar(dec[i % 2][:, r, :], ps[:, 4 + r // 4, (r % 4) * P:(r % 4 + 1) * P], a_s, a_s, ALU.min, ALU.subtract)
                sig_v(ins, row_min)
                yv = y_tm[:, c, g * 512:(g + 1) * 512].rearrange("p (a b) -> p a b", a=HPG)
                ch(v.tensor_tensor(yv, xg, bc(RH("dskip", HEADS)[:, hsl(g)], 2, [P, HPG, HD]), ALU.mult))
                if i >= 1:
                    add_y(i - 1)
                v.wait_ge(dec_ready, i + 1)
                sig_v(v.tensor_tensor(dec[i % 2][:], dec[i % 2][:], bc(cbm[:, c, :], 1, [P, HPG, P]), ALU.mult), m_ready)
                if g >= 1 and c == 0:
                    gate_group(g - 1)
                if g >= 1 and c == 1:
                    scale_group(g - 1)
            add_y(2 * GROUPS - 1)
            gate_group(GROUPS - 1)
            scale_group(GROUPS - 1)
            chain_mark(v, y_ready)
            dve_out(v, 8, COLS["snorm"], U_SOUT, 0, 1)

        def ffn(l, u0):
            dve_norm(v, 1 + 2 * l, COLS[f"ffn{l}"])
            b = l * FT
            w0 = COLS[f"fconv{l}"]

            def tile(j, par, used, v_used):
                src, val = ps[:, par, 0:SEQ], ps[:, par, SEQ:2 * SEQ]
                w = lambda n: cols[:, bass.ds(j * 4 + (w0 + n), 1)]
                k = (j + b) * 3
                v.wait_ge(unit_used, used)
                v.tensor_scalar(fcv[:], src, w(2), w(3), ALU.mult, ALU.add).then_inc(f_chain, 1)
                v.wait_ge(f_chain, k + 1)
                v.scalar_tensor_tensor(fcv[:, 1:SEQ], src[:, 0:SEQ - 1], w(1), fcv[:, 1:SEQ], ALU.mult, ALU.add).then_inc(f_chain, 1)
                v.wait_ge(f_chain, k + 2)
                v.scalar_tensor_tensor(fcv[:, 2:SEQ], src[:, 0:SEQ - 2], w(0), fcv[:, 2:SEQ], ALU.mult, ALU.add).then_inc(f_conv, 1)
                v.wait_ge(f_silu, j + (b + 1))
                v.tensor_tensor(fh32[:], fcv[:], val, ALU.mult).then_inc(f_read, 1)
                v.wait_ge(f_read, j + (b + 1))
                if v_used is not None:
                    v.wait_ge(unit_used, v_used)
                v.tensor_copy(hdh[:, par, :], fh32[:]).then_inc(f_chain, 1)
                v.wait_ge(f_chain, k + 3)
                v.tensor_tensor(hdl[:, par, :], fh32[:], hdh[:, par, :].bitcast(F32), ALU.subtract).then_inc(f_hid, 1)

            tile(0, 0, u0 + 1, None)
            tile(1, 1, u0 + 2, None)
            with nc.vector.Fori(1, FT // 2) as i:
                tile(i * 2, 0, i * 3 + u0, i * 3 + (u0 + 1))
                tile(i * 2 + 1, 1, i * 3 + (u0 + 2), i * 3 + (u0 + 1))
            dve_residual(v, u0 + FFN_UNITS)

        def attention(kind, st, o_dst, gate):
            H, h0 = ATT[kind]
            mla = kind == "mla"
            n0, n1 = (META + P, META + 2 * P) if mla else (P, 2 * P)

            def maxes(n):
                v.wait_ge(s_mm, h0 + n + 1)
                b = 2 + n % 2
                if n >= 4:
                    v.wait_ge(s_exp, h0 + n - 3)
                mx = st[:, 2 * (n % 4):2 * (n % 4) + 2]
                v.tensor_reduce(mx[:, 0:1], ps[:, b, 0:n0], AX.X, ALU.max, negate=True)
                sig_v(v.tensor_reduce(mx[:, 1:2], ps[:, b, n0:n0 + n1], AX.X, ALU.max, negate=True), s_max)

            def turned(n):
                v.wait_ge(pt_filled, h0 + n + 1)
                if mla:
                    if n >= 1:
                        v.wait_ge(o_mm, h0 + n)
                    v.tensor_copy(mpt[0][:, 0:3, :].rearrange("p a b -> p (a b)"), ps[:, 4, 0:384])
                    sig_v(v.tensor_copy(mpt[0][0:META, 3:5, :].rearrange("p a b -> p (a b)"), ps[0:META, 5, 0:256]), pt_evac)
                else:
                    if n >= 2:
                        v.wait_ge(o_mm, h0 + n - 1)
                    sig_v(v.tensor_copy(prt[n % 2][:].rearrange("p a b -> p (a b)"), ps[:, 4, 0:384]), pt_evac)

            def outs(q):
                v.wait_ge(o_mm, h0 + 4 * q + 4)
                b = 6 + q % 2
                sm = st[:, 16 + 8 * q:16 + 8 * q + 8]
                ch(v.reciprocal(sm, sm))
                for t in range(NT):
                    o = o_dst[:, t, q * 256:(q + 1) * 256]
                    ins = v.tensor_tensor(o.rearrange("p (a b) -> p a b", a=4), ps[:, b, t * 256:(t + 1) * 256].rearrange("p (a b) -> p a b", a=4),
                                          sm.rearrange("p (a b) -> p b a", b=2)[:, t, :].unsqueeze(2).broadcast_to([P, 4, HD]), ALU.mult)
                    if t == NT - 1:
                        sig_v(ins, o_evac)
                        v.wait_ge(o_evac, h0 // 4 + q + 1)
                    if gate is not None:
                        if t == 0:
                            ch(ins)
                        ch(v.tensor_tensor(o, o, gate[:, t, q * 256:(q + 1) * 256], ALU.mult))

            for n in range(H):
                maxes(n)
                turned(n)
                if n % 4 == 0 and n >= 4:
                    outs(n // 4 - 1)
            outs(H // 4 - 1)
            chain_mark(v, attn_ready)

        def fox():
            dve_norm(v, 2, COLS["mix1"])
            v.wait_ge(wf_loaded, 16)
            ch(v.tensor_copy(wfh[:], wf[:]))
            sig_v(v.tensor_tensor(wfl[:], wf[:], wfh[:].bitcast(F32), ALU.subtract), wf_split)
            v.wait_ge(f_mm, 1)
            ch(v.tensor_tensor(fst[:, 0], ps[:, 4, 0:32].rearrange("p (a b) -> p a b", a=2), bc(RH("bf", FH), 1, [P, NT, FH]), ALU.add))
            ch(v.tensor_scalar(fst[:, 1], fst[:, 0], -1.0, None, ALU.mult))
            sig_v(v.tensor_tensor(fst[:, 5], fst[:, 0], fst[:, 1], ALU.max), f_abs)
            v.wait_ge(f_l, 1)
            log1p_parts(fst[:, 3], fst[:, 4], fst[:, 6], fst[:, 7])
            ch(v.scalar_tensor_tensor(fst[:, 2], fst[:, 0], 0.0, fst[:, 4], ALU.min, ALU.subtract))
            chain_mark(v, cum_in)
            for n in range(8):
                kind, part = n // 4, n % 4
                v.wait_ge(b_evac, n + 1)
                dst = stat[:, 16 + 32 * kind:48 + 32 * kind].rearrange("p (a b) -> p a b", a=2)[:, :, 4 * part:4 * part + 4]
                sig_v(v.tensor_reduce(dst, tmp[1][:].rearrange("p (t a b) -> p t a b", t=2, a=4), AX.X, ALU.add), b_sq)
            v.wait_ge(b_sq, 8)
            v.wait_ge(cum_mm, 1)
            cum = ps[:, 5, 0:2 * FH].rearrange("p (a b) -> p a b", a=2)
            ch(v.tensor_copy(fq[:, :, :, HD + 1], cum))
            ch(v.tensor_scalar(fk[:, :, :, HD], fq[:, :, :, HD + 1], -1.0, None, ALU.mult))
            ch(v.memset(fq[:, :, :, HD], 1.0))
            ch(v.memset(fk[:, :, :, HD + 1], 1.0))
            for kind, (dst, gain) in enumerate(((fq, "fqg"), (fk, "fkg"))):
                r = stat[:, 16 + 32 * kind:48 + 32 * kind]
                rsqrt(v, ch, r, r, HD)
                if kind == 0:
                    ch(v.tensor_scalar(r, r, HD ** -0.5, None, ALU.mult))
                rv = r.rearrange("p (a b) -> p a b", a=2)
                for t in range(NT):
                    d = dst[:, t, :, 0:HD]
                    ch(v.tensor_tensor(d, d, bc(rv[:, t, :], 2, [P, FH, HD]), ALU.mult))
                    ch(v.tensor_tensor(d, d, bc(RH(gain, HD), 1, [P, FH, HD]), ALU.mult))
            chain_mark(v, qk_ready)
            v.wait_ge(b_evac, 16)
            attention("fox", stat[:, 32:128], xn, fg)
            dve_out(v, 4, None, U_FOUT, 8, 3)

        def mla():
            v.wait_ge(block_ssq, 1)
            rsqrt(v, ch, stat[:, 4:6], stat[:, 0:2], D)
            for t in range(NT):
                ch(v.scalar_tensor_tensor(h[:, t, :], h[:, t, :], stat[:, 4 + t:5 + t], RH("final", D), ALU.mult, ALU.mult))
            chain_mark(v, h_ready)
            ch(v.memset(hc[:, :, 0:HCW - T2], 0.0))
            dve_norm(v, 4, COLS["mix2"])
            for n in range(4):
                v.wait_ge(c_sig, n + 1)
                b = 4 * (n % 2)
                sig_v(v.tensor_tensor(hc[:, n, HCW - T2:], tmp[1][:, 0:T2], ps[:, b, 0:T2], ALU.mult), c_read)
            v.wait_ge(lat_ssq, 5)
            rsqrt(v, ch, mst[:, 40:42], mst[:, 40:42], 256)
            for t in range(NT):
                ch(v.tensor_scalar(tmp[1][:, t * 256:(t + 1) * 256], ps[:, 6, t * 256:(t + 1) * 256], mst[:, 40 + t:41 + t], None, ALU.mult))
            chain_mark(v, lat_n)
            rsqrt(v, ch, mst[0:META, 42:43], mst[0:META, 42:43], P)
            rsqrt(v, ch, mst[:, 43:45], mst[:, 43:45], P)
            for i in range(3):
                m_ = META if i == 0 else P
                ch(v.tensor_scalar(tmp[2][0:m_, i * P:(i + 1) * P], ps[0:m_, 7, i * 160:i * 160 + P], mst[0:m_, 42 + i:43 + i], None, ALU.mult))
                ch(v.tensor_copy(kr[0:m_, i, :], ps[0:m_, 7, i * 160 + P:i * 160 + 160]))
            chain_mark(v, lat_n)
            v.wait_ge(lat_f, 1)
            g0 = COLS["gq"]
            ch(v.tensor_tensor(cqt[:], ps[:, 2, :].rearrange("p (a b) -> p a b", a=2), bc(cols[:, g0:g0 + 2], 2, [P, 2, SEQ]), ALU.mult))
            chain_mark(v, lat_t)
            v.wait_ge(lat_f, 2)
            g0 = COLS["gkv"]
            ch(v.tensor_scalar(ckt[:], ps[:, 3, 0:T2], cols[:, g0:g0 + 1], None, ALU.mult))
            chain_mark(v, lat_t)
            v.wait_ge(mw_loaded, 48)
            v.wait_ge(uq_evac, 2)

            def rotate(x1, x2, cosv, sinv, shape):
                n = int(np.prod(shape[1:]))
                m_ = shape[0]
                names = "p (a b c) -> p a b c" if len(shape) == 4 else "p (a b) -> p a b"
                kw = dict(a=shape[1], b=shape[2]) if len(shape) == 4 else dict(a=shape[1])
                t = [tmp[2 + q // 2][0:m_, (q % 2) * 256:(q % 2) * 256 + n].rearrange(names, **kw) for q in range(4)]
                ch(v.tensor_tensor(t[0], x1, cosv, ALU.mult))
                ch(v.tensor_tensor(t[1], x2, sinv, ALU.mult))
                ch(v.tensor_tensor(t[2], x2, cosv, ALU.mult))
                ch(v.tensor_tensor(t[3], x1, sinv, ALU.mult))
                ch(v.tensor_tensor(x1, t[0], t[1], ALU.subtract))
                ch(v.tensor_tensor(x2, t[2], t[3], ALU.add))

            cq_ = lambda n: cs[:, 1:3, n, :].unsqueeze(2).broadcast_to([P, NT, MH, 16])
            rotate(mq[:, :, :, NOPE:NOPE + 16], mq[:, :, :, NOPE + 16:QD], cq_(0), cq_(1), [P, NT, MH, 16])
            rotate(kr[:, 1:3, 0:16], kr[:, 1:3, 16:32], cs[:, 1:3, 0, :], cs[:, 1:3, 1, :], [P, 2, 16])
            rotate(kr[0:META, 0:1, 0:16], kr[0:META, 0:1, 16:32], cs[0:META, 0:1, 0, :], cs[0:META, 0:1, 1, :], [META, 1, 16])
            v.wait_ge(ukv_evac, 3)
            ch(v.tensor_copy(mk[0:META, 0, :, NOPE:QD], kr[0:META, 0, :].unsqueeze(1).broadcast_to([META, MH, ROPE])))
            for t in range(NT):
                ch(v.tensor_copy(mk[:, 1 + t, :, NOPE:QD], bc(kr[:, 1 + t, :], 1, [P, MH, ROPE])))
            chain_mark(v, mqk_ready)
            w0 = COLS["cconv"]

            def taps(k):
                for c in range(CT):
                    w = cols[:, w0 + 32 * c + k:w0 + 32 * c + k + 1]
                    if k == 0:
                        ins = v.tensor_scalar(ca[:, c, :], hc[:, c, 0:SEQ], w, cols[:, w0 + 32 * c + 31:w0 + 32 * c + 32], ALU.mult, ALU.add)
                    else:
                        ins = v.scalar_tensor_tensor(ca[:, c, :], hc[:, c, k:k + SEQ], w, ca[:, c, :], ALU.mult, ALU.add)
                ch(ins)

            state = {"k": 0}

            def some_taps(n):
                for _ in range(n):
                    if state["k"] < CONV_K:
                        taps(state["k"])
                        state["k"] += 1

            H, h0 = ATT["mla"]
            v.wait_ge(c_read, 4)
            attention_with(some_taps)
            some_taps(CONV_K)
            chain_mark(v, conv_done)
            v.wait_ge(ct_mm, 1)
            for t in range(NT):
                bn, ag = stat[:, 16:22], stat[:, 24:26]
                ch(v.bn_stats(bn, ps[:, t, :]))
                ch(v.bn_aggr(ag, bn))
                rsqrt(v, ch, stat[:, 26:27], ag[:, 1:2], 1)
                m = mix[:, t, 512:1024]
                ch(v.tensor_scalar(m, ps[:, t, :], ag[:, 0:1], stat[:, 26:27], ALU.subtract, ALU.mult))
                ch(v.tensor_tensor(m, m, RH("lng", 512), ALU.mult))
                sig_v(v.tensor_tensor(m, m, RH("lnb", 512), ALU.add), ln_ready)
            v.wait_ge(mix_ssq, 1)
            rsqrt(v, ch, mst[:, 48:52], mst[:, 48:52], 512)
            for t in range(NT):
                for half in range(2):
                    m = mix[:, t, half * 512:(half + 1) * 512]
                    q = 48 + 2 * t + half
                    ch(v.tensor_scalar(m, m, mst[:, q:q + 1], None, ALU.mult))
            chain_mark(v, mix_ready)
            dve_out(v, 4, COLS["gout"], U_MOUT, 12, 6)

        def attention_with(filler):
            H, h0 = ATT["mla"]
            st = mst
            n0, n1 = META + P, META + 2 * P
            for n in range(H):
                v.wait_ge(s_mm, h0 + n + 1)
                b = 2 + n % 2
                mx = st[:, 2 * (n % 4):2 * (n % 4) + 2]
                v.tensor_reduce(mx[:, 0:1], ps[:, b, 0:n0], AX.X, ALU.max, negate=True)
                sig_v(v.tensor_reduce(mx[:, 1:2], ps[:, b, n0:n0 + n1], AX.X, ALU.max, negate=True), s_max)
                filler(2)
                v.wait_ge(pt_filled, h0 + n + 1)
                if n >= 1:
                    v.wait_ge(o_mm, h0 + n)
                v.tensor_copy(mpt[0][:, 0:3, :].rearrange("p a b -> p (a b)"), ps[:, 4, 0:384])
                sig_v(v.tensor_copy(mpt[0][0:META, 3:5, :].rearrange("p a b -> p (a b)"), ps[0:META, 5, 0:256]), pt_evac)
                filler(2)
            for q in range(H // 4):
                v.wait_ge(o_mm, h0 + 4 * q + 4)
                sm = st[:, 16 + 8 * q:16 + 8 * q + 8]
                ch(v.reciprocal(sm, sm))
                for t in range(NT):
                    o = mix[:, t, q * 256:(q + 1) * 256]
                    ch(v.tensor_tensor(o.rearrange("p (a b) -> p a b", a=4), ps[:, 6 + q % 2, t * 256:(t + 1) * 256].rearrange("p (a b) -> p a b", a=4),
                                       sm.rearrange("p (a b) -> p b a", b=2)[:, t, :].unsqueeze(2).broadcast_to([P, 4, HD]), ALU.mult))
            chain_mark(v, attn_ready)

        def routing():
            ch(v.memset(keys[:], 0.0))
            chain_mark(v, keys_z)
            dve_norm(v, 5, COLS["ffn2"])
            LOW = -3.0e38

            def top16(rows_of):
                lag = chains["v"].lag
                for step in (lambda vals, tops, idx: v.max(tops[:, 0:8], vals),
                             lambda vals, tops, idx: v.max_index(idx[:, 0:8], tops[:, 0:8], vals),
                             lambda vals, tops, idx: v.match_replace(vals, tops[:, 0:8], vals, LOW),
                             lambda vals, tops, idx: v.max(tops[:, 8:16], vals),
                             lambda vals, tops, idx: v.max_index(idx[:, 8:16], tops[:, 8:16], vals)):
                    for row in rows_of:
                        lag(step(*row))

            for t in range(NT):
                for n in range(0, 2 * PH, 2):
                    v.wait_ge(sc_evac, 4 * t + n // 4 + 1)
                    top16([(sc[:, t, i, :], sv[:, t, i, :], si[:, t, i, :]) for i in (n, n + 1)])
            chains["v"].settle()
            ch(v.tensor_copy(sif[:], si[:]))
            half = lambda buf, t, p: buf[:, t].rearrange("p (h two) k -> p h two k", two=2)[:, :, p, :]
            for t in range(NT):
                c4 = cand[:, t].rearrange("p h (a b) -> p h a b", a=TOPK)
                ch(v.tensor_tensor(c4, half(sv, t, 0).unsqueeze(3).broadcast_to([P, PH, TOPK, TOPK]),
                                   half(sv, t, 1).unsqueeze(2).broadcast_to([P, PH, TOPK, TOPK]), ALU.add))
                for n in range(0, PH, 2):
                    top16([(cand[:, t, i, :], tv[:, t, i, :], ts[:, t, i, :]) for i in (n, n + 1)])
            chains["v"].settle()
            tvf = tv[:].rearrange("p t h k -> p (t h) k")
            ch(v.tensor_copy(stat[:, 16:32], tvf[:, :, 0]))
            sig_v(v.tensor_tensor(tvf, tvf, bc(stat[:, 16:32], 2, [P, NT * PH, TOPK]), ALU.subtract), tv_sub)
            ch(v.tensor_scalar(tau[:], ts[:], 4, None, ALU.logical_shift_right))
            ch(v.tensor_scalar(tbu[:], ts[:], 15, None, ALU.bitwise_and))
            ch(v.tensor_copy(taf[:], tau[:]))
            ch(v.tensor_copy(tbf[:], tbu[:]))
            v.wait_ge(tv_exp, 1)
            ch(v.tensor_reduce(stat[:, 16:32], tvf, AX.X, ALU.add))
            ch(v.reciprocal(stat[:, 16:32], stat[:, 16:32]))
            ch(v.tensor_tensor(tvf, tvf, bc(stat[:, 16:32], 2, [P, NT * PH, TOPK]), ALU.mult))
            for t in range(NT):
                for p, pick in ((0, taf), (1, tbf)):
                    want = pick[:, t].rearrange("p h k -> p (h k)").unsqueeze(2).broadcast_to([P, PH * TOPK, TOPK])
                    ch(v.tensor_tensor(eq[:], want, iota[:, 0:TOPK].unsqueeze(1).broadcast_to([P, PH * TOPK, TOPK]), ALU.is_equal))
                    e4 = eq[:].rearrange("p (h k) a -> p h k a", h=PH)
                    ch(v.tensor_tensor(e4, e4, half(sif, t, p).unsqueeze(2).broadcast_to([P, PH, TOPK, TOPK]), ALU.mult))
                    ch(v.tensor_reduce(sif_sel[p][:, t].rearrange("p a b -> p (a b)"), eq[:], AX.X, ALU.add))
            chain_mark(v, lst_in)
            v.wait_ge(lst_mm, 1)
            v.wait_ge(h_saved, 16)
            for w in range(3):
                ch(v.tensor_copy(lst[:, w, :], ps[:, w, 0:SEQ]))
            chain_mark(v, lst_out)

        def experts():
            def second_u(m):
                v.wait_ge(hi_u_done, m + 1)
                v.tensor_tensor(lo[0][:], raw[0][:], hi[0][:].bitcast(F32), ALU.subtract).then_inc(lo_u_done, 1)

            def second_v(m):
                v.wait_ge(hi_v_done, m + 1)
                v.tensor_tensor(lo[1][:], raw[1][:], hi[1][:].bitcast(F32), ALU.subtract).then_inc(lo_v_done, 1)

            second_u(0)
            def one_hots(n, b):
                for w, places in ((1, oj), (0, oi)):
                    number = lst[:, w, bass.ds(n * GT, GT)].unsqueeze(2).broadcast_to([P, GT, P])
                    v.tensor_tensor(places[b][:], iota[:].unsqueeze(1).broadcast_to([P, GT, P]), number,
                                    ALU.is_equal).then_inc((row_hot, col_hot)[w], 1)

            for n in range(3):
                one_hots(n, n)
            v.wait_ge(g_mm, 2)
            one_hots(3, 0)
            v.wait_ge(g_mm, 4)
            one_hots(4, 1)
            with nc.vector.Fori(0, (GROUPS_OF_TOKENS - 5) // 3) as i:
                for k in range(3):
                    v.wait_ge(g_mm, i * 6 + (2 * k + 6))
                    one_hots(i * 3 + (5 + k), (5 + k) % 3)

            def weigh(m):
                mm = m * 2 if not isinstance(m, int) else 2 * m
                v.wait_ge(a_gelu, m + 1)
                v.tensor_tensor(gl[:].rearrange("p a b -> p (a b)"), gl[:].rearrange("p a b -> p (a b)"),
                                gates[:, bass.ds(mm, 2), :].rearrange("p a b -> p (a b)"), ALU.mult).then_inc(w_mul, 1)

            def parts(m, used):
                v.wait_ge(w_mul, m + 1)
                if used is not None:
                    v.wait_ge(unit_used, used)
                v.tensor_copy(wgh[:], gl[:]).then_inc(p_chain, 1)
                v.wait_ge(p_chain, m + 1)
                v.tensor_tensor(wgl[:], gl[:], wgh[:].bitcast(F32), ALU.subtract).then_inc(w_ready, 1)

            v.wait_ge(g_evac, SEQ // 4)
            weigh(0)
            second_u(1)
            parts(0, None)
            second_v(0)
            with nc.vector.Fori(1, PAIRS - 1) as m:
                weigh(m)
                second_u(m + 1)
                parts(m, m * 2 + (U_PEER + 1))
                second_v(m)
            weigh(PAIRS - 1)
            parts(PAIRS - 1, U_PEER + 2 * PAIRS - 1)
            second_v(PAIRS - 1)
            v.wait_ge(h_back, 32)
            v.wait_ge(unit_used, U_PEER + 2 * PAIRS)
            for t in range(NT):
                for n in range(2):
                    hs = hf[:, t, n * 512:(n + 1) * 512]
                    ch(v.tensor_tensor(hs, hs, ps[:, 4 + 2 * t + n, :], ALU.add))
            chain_mark(v, h_ready)
            v.wait_ge(fin_ssq, 1)
            rsqrt(v, ch, stat[:, 4:6], stat[:, 0:2], D)
            for t in range(NT):
                ch(v.scalar_tensor_tensor(fo[:, t, :], hf[:, t, :], stat[:, 4 + t:5 + t], gfin[:], ALU.mult, ALU.mult))
            chain_mark(v, fin_ready)

        ssd()
        ffn(0, U_FFN0)
        fox()
        ffn(1, U_FFN1)
        mla()
        routing()
        experts()

    block_cm.__exit__(None, None, None)


def kernel(**inputs):
    import concourse.bacc as _bacc
    from concourse.bass_utils import run_bass_kernel_spmd as _run

    a = {k: np.asarray(v) for k, v in inputs.items()}

    def by_columns(w, order=None):
        return w.reshape(KC, P, -1, 256).transpose(2, 1, 0, 3).reshape(-1, P, UNIT)

    def by_rows(w):
        return w.reshape(-1, 2, P, D).transpose(0, 2, 1, 3).reshape(-1, P, UNIT)

    def paired(w, half):
        return w.reshape(D, 2, half // P, P).transpose(0, 2, 1, 3).reshape(D, 2 * half)

    def chunks(vec):
        return vec.reshape(-1, P).T

    w_in = a["ssd_w_in"][0]
    z, xbc, w_dt = w_in[:, :INNER], w_in[:, INNER:INNER + 3072], w_in[:, INNER + 3072:]
    xbc = np.concatenate([xbc[:, INNER:], xbc[:, :INNER]], axis=1)
    fox = a["fox_w_in"][0]
    w2 = a["w_in_2"][0]
    lat = np.concatenate([w2[:, 1024:1440], np.zeros((D, 96), w2.dtype)], axis=1)
    small = lambda w: w.reshape(KC, P, -1).transpose(1, 0, 2)
    pos = np.arange(T2, dtype=np.float32)
    freqs = (np.float32(10000.0) ** (-np.arange(16, dtype=np.float32) / np.float32(16))).astype(np.float32)
    ang = (pos[:, None] * freqs[None, :]).astype(np.float32)
    cs = np.zeros((P, 3, 2, 16), np.float32)
    for n, f in enumerate((np.cos, np.sin)):
        tab = f(ang).astype(np.float32)
        cs[:META, 0, n] = tab[:META]
        cs[:, 1, n] = tab[META:META + P]
        cs[:, 2, n] = tab[META + P:]
    conv = lambda w, b: np.concatenate([w, b[None]], axis=0).reshape(w.shape[0] + 1, -1, P).transpose(2, 1, 0).reshape(P, -1)
    cols = np.concatenate(
        [chunks(a["mix_norm_g"][0]), chunks(a["ffn_norm_g"][0]), chunks(a["mix_norm_g"][1]), chunks(a["ffn_norm_g"][1]),
         chunks(a["g_mix_norm_2"][0]), chunks(a["g_ffn_norm_2"][0]),
         conv(a["ssd_conv_w"][0], a["ssd_conv_b"][0]), chunks(a["ssd_norm_g"][0]),
         conv(a["ffn_conv_w"][0], a["ffn_conv_b"][0]), conv(a["ffn_conv_w"][1], a["ffn_conv_b"][1]),
         conv(a["conv_w_2"][0], a["conv_b_2"][0]),
         chunks(a["g_out_attn_2"][0]), chunks(a["g_out_conv_2"][0]), chunks(a["g_q_2"][0]), chunks(a["g_kv_2"][0])], axis=1)
    rows = np.concatenate([a["ssd_dt_bias"][0], a["ssd_a_log"][0], a["ssd_d"][0], a["fox_b_f"][0], a["fox_q_norm_g"][0],
                           a["fox_k_norm_g"][0], a["g_conv_ln_2"][0], a["b_conv_ln_2"][0], a["final_norm_g"]])[None]
    u = a["peer_u_2"][0].reshape(P, PAIRS, 2, KC, P).transpose(1, 4, 3, 2, 0).reshape(PAIRS, P, UNIT)
    vt = a["peer_v_2"][0].reshape(P, PAIRS, 2, D).transpose(1, 0, 2, 3).reshape(PAIRS, P, UNIT)
    arrays = {
        "x": a["x"], "cols": cols, "rows": rows, "w_dt": small(w_dt), "w_f": small(fox[:, 4096:]),
        "w_xbc": by_columns(xbc), "w_z": by_columns(z), "w_sout": by_rows(a["ssd_w_out"][0]),
        "w_fox": by_columns(fox[:, :4096]), "w_fout": by_rows(a["fox_w_out"][0]),
        "w_conv": by_columns(paired(w2[:, :1024], 512)), "w_lat": by_columns(lat),
        "w_mout": by_rows(a["w_out_2"][0]), "w_wq": by_columns(a["peer_wq_2"][0]),
        "w_uq": a["w_uq_2"][0].reshape(2, P, -1).transpose(1, 0, 2), "w_ukv": a["w_ukv_2"][0],
        "meta": a["meta_2"], "cs": cs, "keys": a["peer_keys_2"][0].transpose(1, 3, 0, 2),
        "w_u": u, "w_v": vt, "gfin": a["g_final_2"][None],
    }
    for l in range(2):
        arrays[f"w_up{l}"] = by_columns(paired(a["ffn_w_up"][l], 2816))
        arrays[f"w_down{l}"] = by_rows(a["ffn_w_down"][l])
    arrays = {k: np.ascontiguousarray(v) for k, v in arrays.items()}
    nc = _bacc.Bacc("TRN2", target_bir_lowering=False, num_devices=1)
    A = {k: nc.dram_tensor(f"in_{k}", v.shape, F32, kind="ExternalInput").ap() for k, v in arrays.items()}
    out = nc.dram_tensor("out_0", (1, SEQ, D), F32, kind="ExternalOutput").ap()
    build(nc, A, out)
    r = _run(nc, [{f"in_{k}": v for k, v in arrays.items()}], core_ids=[0])
    return r.results[0]["out_0"]
```
